# Optimizing a Trainium2 kernel written in Bass

```python
import jax, jax.numpy as jnp
from jax import lax
import numpy as np

D_MODEL = 1024
BATCH = 1
SEQ = 128
DEPTH = 2
DEC_BATCH = 1
DEC_SEQ = 256
PAST_LEN = 128

GRID_W = 64
HEAD_DIM = 64
NA_HEADS = 4
NA_WIN_H = 8
NA_WIN_W = 16
MLA_HEADS = 6
MLA_Q_RANK = 256
MLA_KV_RANK = 128
MLA_NOPE_DIM = 64
MLA_ROPE_DIM = 32
MLA_V_DIM = 64
MLA_QK_DIM = MLA_NOPE_DIM + MLA_ROPE_DIM
SWA_HEADS = 6
SWA_KV_HEADS = 2
SWA_WINDOW = 128
ROPE_BASE = 10000.0
Q_BLOCK = 128
N_EXPERTS = 16
N_EXPERT_GROUPS = 4
EXPERTS_PER_GROUP = N_EXPERTS // N_EXPERT_GROUPS
TOP_K = 2
D_EXPERT = 512
RMS_EPS = 1e-6
N_MOD = 6

NA_IN = 3 * NA_HEADS * HEAD_DIM
MLA_IN = MLA_Q_RANK + MLA_KV_RANK + MLA_ROPE_DIM
SWA_IN = (SWA_HEADS + 2 * SWA_KV_HEADS) * HEAD_DIM
IN_WIDTH = NA_IN + MLA_IN + SWA_IN
MIX_WIDTH = NA_HEADS * HEAD_DIM + MLA_HEADS * MLA_V_DIM + SWA_HEADS * HEAD_DIM

kernel_name = "hybrid_prefix_flow_trunk_step"

def rms_norm(x, g):
    xf = x.astype(jnp.float32)
    y = xf * lax.rsqrt(jnp.mean(xf * xf, axis=-1, keepdims=True) + RMS_EPS)
    return (y * g.astype(jnp.float32)).astype(x.dtype)

def ada_mod(cond, w_ada_l, b_ada_l):
    m = jax.nn.silu(cond) @ w_ada_l + b_ada_l
    m = m.reshape(cond.shape[0], 1, N_MOD, D_MODEL)
    return [m[:, :, i] for i in range(N_MOD)]

def axial_rope(T, rot_dim):
    t = jnp.arange(T, dtype=jnp.int32)
    row = (t // GRID_W).astype(jnp.float32)
    col = (t % GRID_W).astype(jnp.float32)
    per_axis = rot_dim // 2
    inv = ROPE_BASE ** (-jnp.arange(0, per_axis, 2, dtype=jnp.float32) / per_axis)
    ang = jnp.concatenate([row[:, None] * inv, col[:, None] * inv], axis=-1)
    return jnp.cos(ang), jnp.sin(ang)

def apply_rope(x, cos, sin):
    half = x.shape[-1] // 2
    x1, x2 = x[..., :half], x[..., half:]
    cs = cos[None, :, None, :].astype(x.dtype)
    sn = sin[None, :, None, :].astype(x.dtype)
    return jnp.concatenate([x1 * cs - x2 * sn, x2 * cs + x1 * sn], axis=-1)

def block_attention(q, k, v, sink=None):
    B, Tq, H, dk = q.shape
    Hk = k.shape[2]
    G = H // Hk
    dv = v.shape[-1]
    nb = Tq // Q_BLOCK
    qb = q.reshape(B, nb, Q_BLOCK, Hk, G, dk).transpose(1, 0, 2, 3, 4, 5)
    scale = dk ** -0.5

    def one_block(qblk):
        s = jnp.einsum('bqkgd,bskd->bkgqs', qblk, k, preferred_element_type=jnp.float32) * scale
        if sink is not None:
            s_sink = jnp.broadcast_to(sink.astype(jnp.float32).reshape(1, Hk, G, 1, 1), s.shape[:-1] + (1,))
            s = jnp.concatenate([s, s_sink], axis=-1)
        p = jax.nn.softmax(s, axis=-1)
        if sink is not None:
            p = p[..., :-1]
        return jnp.einsum('bkgqs,bskd->bqkgd', p.astype(v.dtype), v)

    o = lax.map(one_block, qb)
    return o.transpose(1, 0, 2, 3, 4, 5).reshape(B, Tq, H, dv)

def neighborhood_attention(q, k, v, ck, cv, rpb):
    B, T, H, D = q.shape
    rows = T // GRID_W
    kh = min(NA_WIN_H, rows)
    W = GRID_W
    kw = NA_WIN_W
    qg = q.reshape(B, rows, W, H, D)
    kg = k.reshape(B, rows, W, H, D)
    vg = v.reshape(B, rows, W, H, D)
    r = jnp.arange(rows)
    row_start = jnp.clip(r - kh // 2, 0, rows - kh)
    row_idx = row_start[:, None] + jnp.arange(kh)[None, :]
    k_nb = kg[:, row_idx]
    v_nb = vg[:, row_idx]
    cidx = jnp.arange(W)
    col_start = jnp.clip(cidx - kw // 2, 0, W - kw)
    col_ok = (cidx[None, :] >= col_start[:, None]) & (cidx[None, :] < col_start[:, None] + kw)
    dr = row_idx - r[:, None] + (NA_WIN_H - 1)
    dc = jnp.clip(cidx[None, :] - cidx[:, None] + (kw - 1), 0, 2 * kw - 2)
    bias = rpb[:, dr[:, :, None, None], dc[None, None]]
    bias = bias.transpose(0, 1, 3, 2, 4).astype(jnp.float32)
    scale = D ** -0.5
    s_nb = jnp.einsum('brqhd,brkwhd->bhrqkw', qg, k_nb, preferred_element_type=jnp.float32) * scale + bias[None]
    s_nb = jnp.where(col_ok[None, None, None, :, None, :], s_nb, -jnp.inf)
    s_nb = s_nb.reshape(B, H, rows, W, kh * W)
    s_ctx = jnp.einsum('brqhd,blhd->bhrql', qg, ck, preferred_element_type=jnp.float32) * scale
    p = jax.nn.softmax(jnp.concatenate([s_nb, s_ctx], axis=-1), axis=-1)
    p_nb = p[..., :kh * W].reshape(B, H, rows, W, kh, W).astype(v.dtype)
    p_ctx = p[..., kh * W:].astype(cv.dtype)
    o = jnp.einsum('bhrqkw,brkwhd->brqhd', p_nb, v_nb) + jnp.einsum('bhrql,blhd->brqhd', p_ctx, cv)
    return o.reshape(B, T, H, D)

def banded_window_attention(q, k, v, ck, cv, sink):
    B, T, H, D = q.shape
    Hk = k.shape[2]
    G = H // Hk
    Bk = SWA_WINDOW
    nb = T // Bk
    L = ck.shape[1]
    qb = q.reshape(B, nb, Bk, Hk, G, D)
    pad = ((0, 0), (Bk, Bk), (0, 0), (0, 0))
    kp = jnp.pad(k, pad).reshape(B, nb + 2, Bk, Hk, D)
    vp = jnp.pad(v, pad).reshape(B, nb + 2, Bk, Hk, D)
    kb = jnp.concatenate([kp[:, :-2], kp[:, 1:-1], kp[:, 2:]], axis=2)
    vb = jnp.concatenate([vp[:, :-2], vp[:, 1:-1], vp[:, 2:]], axis=2)
    qi = jnp.arange(Bk)
    kj = jnp.arange(3 * Bk)
    rel = kj[None, :] - qi[:, None]
    band = (rel >= 0) & (rel <= 2 * Bk)
    kpos = jnp.arange(nb)[:, None] * Bk - Bk + kj[None, :]
    inside = (kpos >= 0) & (kpos < T)
    mask = band[None] & inside[:, None, :]
    scale = D ** -0.5
    s_loc = jnp.einsum('bnqkgd,bnskd->bnkgqs', qb, kb, preferred_element_type=jnp.float32) * scale
    s_loc = jnp.where(mask[None, :, None, None], s_loc, -jnp.inf)
    s_ctx = jnp.einsum('bnqkgd,blkd->bnkgql', qb, ck, preferred_element_type=jnp.float32) * scale
    s_sink = jnp.broadcast_to(sink.astype(jnp.float32).reshape(1, 1, Hk, G, 1, 1), s_loc.shape[:-1] + (1,))
    p = jax.nn.softmax(jnp.concatenate([s_loc, s_ctx, s_sink], axis=-1), axis=-1)
    p_loc = p[..., :3 * Bk].astype(v.dtype)
    p_ctx = p[..., 3 * Bk:3 * Bk + L].astype(cv.dtype)
    o = jnp.einsum('bnkgqs,bnskd->bnqkgd', p_loc, vb) + jnp.einsum('bnkgql,blkd->bnqkgd', p_ctx, cv)
    return o.reshape(B, T, H, D)

def project(h, w_in_l, g_q, w_qb, g_kv):
    B, T, _ = h.shape
    z = h @ w_in_l
    na = z[..., :NA_IN].reshape(B, T, 3, NA_HEADS, HEAD_DIM)
    o = NA_IN
    cq = z[..., o:o + MLA_Q_RANK]
    o += MLA_Q_RANK
    ckv = z[..., o:o + MLA_KV_RANK]
    o += MLA_KV_RANK
    kpe = z[..., o:o + MLA_ROPE_DIM]
    o += MLA_ROPE_DIM
    sw = z[..., o:].reshape(B, T, SWA_HEADS + 2 * SWA_KV_HEADS, HEAD_DIM)
    mla_q = (rms_norm(cq, g_q) @ w_qb).reshape(B, T, MLA_HEADS, MLA_QK_DIM)
    ckv = rms_norm(ckv, g_kv)
    return (na[:, :, 0], na[:, :, 1], na[:, :, 2], mla_q, ckv, kpe,
            sw[:, :, :SWA_HEADS], sw[:, :, SWA_HEADS:SWA_HEADS + SWA_KV_HEADS], sw[:, :, SWA_HEADS + SWA_KV_HEADS:])

def mla_expand(ckv, kpe, w_kvb):
    B, T, _ = ckv.shape
    kv = (ckv @ w_kvb).reshape(B, T, MLA_HEADS, MLA_NOPE_DIM + MLA_V_DIM)
    k_nope, v = kv[..., :MLA_NOPE_DIM], kv[..., MLA_NOPE_DIM:]
    k = jnp.concatenate([k_nope, jnp.broadcast_to(kpe[:, :, None, :], (B, T, MLA_HEADS, MLA_ROPE_DIM))], axis=-1)
    return k, v

def merge_heads(o_na, o_mla, o_swa, w_out_l):
    B, T = o_na.shape[:2]
    o = jnp.concatenate([o_na.reshape(B, T, -1), o_mla.reshape(B, T, -1), o_swa.reshape(B, T, -1)], axis=-1)
    return o @ w_out_l

def moe(h, w_router, b_router, w_gate, w_up, w_down):
    B, T, Dm = h.shape
    t = h.reshape(B * T, Dm)
    scores = jax.nn.sigmoid(jnp.einsum('nd,de->ne', t, w_router, preferred_element_type=jnp.float32))
    sel = (scores + b_router.astype(jnp.float32)).reshape(-1, N_EXPERT_GROUPS, EXPERTS_PER_GROUP)
    group_score = jnp.sum(lax.top_k(sel, TOP_K)[0], axis=-1)
    best = jnp.argmax(group_score, axis=-1)
    in_group = jnp.take_along_axis(sel, best[:, None, None], axis=1)[:, 0]
    _, local = lax.top_k(in_group, TOP_K)
    idx = best[:, None] * EXPERTS_PER_GROUP + local
    w = jnp.take_along_axis(scores, idx, axis=1)
    w = w / jnp.sum(w, axis=-1, keepdims=True)
    gate = jnp.sum(jax.nn.one_hot(idx, N_EXPERTS, dtype=jnp.float32) * w[..., None], axis=1)
    hg = jnp.einsum('nd,edf->nef', t, w_gate)
    hu = jnp.einsum('nd,edf->nef', t, w_up)
    a = jax.nn.silu(hg) * hu * gate[..., None].astype(t.dtype)
    y = jnp.einsum('nef,efd->nd', a, w_down)
    return y.reshape(B, T, Dm)

def setup_inputs(seed: int = 0) -> dict:
    key = jax.random.key(seed)
    ks = jax.random.split(key, 32)
    f32 = jnp.float32

    def nrm(k, shape, s):
        return jax.random.normal(k, shape, f32) * s

    return {
        'x_prompt': nrm(ks[0], (BATCH, SEQ, D_MODEL), 1.0),
        'x_sample': nrm(ks[1], (DEC_BATCH, DEC_SEQ, D_MODEL), 1.0),
        'c': nrm(ks[2], (DEC_BATCH, D_MODEL), 1.0),
        'cache_na_k': nrm(ks[3], (DEC_BATCH, DEPTH, PAST_LEN, NA_HEADS, HEAD_DIM), 1.0),
        'cache_na_v': nrm(ks[4], (DEC_BATCH, DEPTH, PAST_LEN, NA_HEADS, HEAD_DIM), 1.0),
        'cache_mla_ckv': nrm(ks[5], (DEC_BATCH, DEPTH, PAST_LEN, MLA_KV_RANK), 1.0),
        'cache_mla_kpe': nrm(ks[6], (DEC_BATCH, DEPTH, PAST_LEN, MLA_ROPE_DIM), 1.0),
        'cache_swa_k': nrm(ks[7], (DEC_BATCH, DEPTH, PAST_LEN, SWA_KV_HEADS, HEAD_DIM), 1.0),
        'cache_swa_v': nrm(ks[8], (DEC_BATCH, DEPTH, PAST_LEN, SWA_KV_HEADS, HEAD_DIM), 1.0),
        'c_ctx': nrm(ks[9], (D_MODEL,), 1.0),
        'w_ada': nrm(ks[10], (DEPTH, D_MODEL, N_MOD * D_MODEL), 0.5 * D_MODEL ** -0.5),
        'b_ada': nrm(ks[11], (DEPTH, N_MOD * D_MODEL), 0.01),
        'g_attn': 1.0 + nrm(ks[12], (DEPTH, D_MODEL), 0.05),
        'w_in': nrm(ks[13], (DEPTH, D_MODEL, IN_WIDTH), D_MODEL ** -0.5),
        'g_mla_q': 1.0 + nrm(ks[14], (DEPTH, MLA_Q_RANK), 0.05),
        'w_mla_qb': nrm(ks[15], (DEPTH, MLA_Q_RANK, MLA_HEADS * MLA_QK_DIM), MLA_Q_RANK ** -0.5),
        'g_mla_kv': 1.0 + nrm(ks[16], (DEPTH, MLA_KV_RANK), 0.05),
        'w_mla_kvb': nrm(ks[17], (DEPTH, MLA_KV_RANK, MLA_HEADS * (MLA_NOPE_DIM + MLA_V_DIM)), MLA_KV_RANK ** -0.5),
        'na_rpb': nrm(ks[18], (DEPTH, NA_HEADS, 2 * NA_WIN_H - 1, 2 * NA_WIN_W - 1), 0.2),
        'swa_sink': nrm(ks[19], (DEPTH, SWA_HEADS), 0.5),
        'w_out': nrm(ks[20], (DEPTH, MIX_WIDTH, D_MODEL), MIX_WIDTH ** -0.5),
        'g_ffn': 1.0 + nrm(ks[21], (DEPTH, D_MODEL), 0.05),
        'w_router': nrm(ks[22], (D_MODEL, N_EXPERTS), D_MODEL ** -0.5),
        'b_router': nrm(ks[23], (N_EXPERTS,), 0.01),
        'w_gate': nrm(ks[24], (DEPTH, N_EXPERTS, D_MODEL, D_EXPERT), D_MODEL ** -0.5),
        'w_up': nrm(ks[25], (DEPTH, N_EXPERTS, D_MODEL, D_EXPERT), D_MODEL ** -0.5),
        'w_down': nrm(ks[26], (DEPTH, N_EXPERTS, D_EXPERT, D_MODEL), D_EXPERT ** -0.5),
        'g_final': 1.0 + nrm(ks[27], (D_MODEL,), 0.05),
    }

def reference(x_prompt, x_sample, c, cache_na_k, cache_na_v, cache_mla_ckv, cache_mla_kpe, cache_swa_k, cache_swa_v,
              c_ctx, w_ada, b_ada, g_attn, w_in, g_mla_q, w_mla_qb, g_mla_kv, w_mla_kvb, na_rpb, swa_sink, w_out,
              g_ffn, w_router, b_router, w_gate, w_up, w_down, g_final):
    y = x_prompt
    na_ks, na_vs, ckvs, kpes, sw_ks, sw_vs = [], [], [], [], [], []
    for l in range(DEPTH):
        sh1, sc1, gt1, sh2, sc2, gt2 = ada_mod(c_ctx[None], w_ada[l], b_ada[l])
        h = rms_norm(y, g_attn[l]) * (1 + sc1) + sh1
        na_q, na_k, na_v, mla_q, ckv, kpe, sw_q, sw_k, sw_v = project(h, w_in[l], g_mla_q[l], w_mla_qb[l], g_mla_kv[l])
        mla_k, mla_v = mla_expand(ckv, kpe, w_mla_kvb[l])
        o = merge_heads(block_attention(na_q, na_k, na_v),
                        block_attention(mla_q, mla_k, mla_v),
                        block_attention(sw_q, sw_k, sw_v, swa_sink[l]), w_out[l])
        y = y + gt1 * o
        h = rms_norm(y, g_ffn[l]) * (1 + sc2) + sh2
        y = y + gt2 * moe(h, w_router, b_router, w_gate[l], w_up[l], w_down[l])
        na_ks.append(na_k)
        na_vs.append(na_v)
        ckvs.append(ckv)
        kpes.append(kpe)
        sw_ks.append(sw_k)
        sw_vs.append(sw_v)
    y_prompt = rms_norm(y, g_final)
    new_na_k = jnp.stack(na_ks, axis=1)
    new_na_v = jnp.stack(na_vs, axis=1)
    new_mla_ckv = jnp.stack(ckvs, axis=1)
    new_mla_kpe = jnp.stack(kpes, axis=1)
    new_swa_k = jnp.stack(sw_ks, axis=1)
    new_swa_v = jnp.stack(sw_vs, axis=1)

    T = x_sample.shape[1]
    cos_m, sin_m = axial_rope(T, MLA_ROPE_DIM)
    cos_s, sin_s = axial_rope(T, HEAD_DIM)
    z = x_sample
    for l in range(DEPTH):
        sh1, sc1, gt1, sh2, sc2, gt2 = ada_mod(c, w_ada[l], b_ada[l])
        h = rms_norm(z, g_attn[l]) * (1 + sc1) + sh1
        na_q, na_k, na_v, mla_q, ckv, kpe, sw_q, sw_k, sw_v = project(h, w_in[l], g_mla_q[l], w_mla_qb[l], g_mla_kv[l])
        o_na = neighborhood_attention(na_q, na_k, na_v, cache_na_k[:, l], cache_na_v[:, l], na_rpb[l])
        mla_q = jnp.concatenate([mla_q[..., :MLA_NOPE_DIM], apply_rope(mla_q[..., MLA_NOPE_DIM:], cos_m, sin_m)], axis=-1)
        kpe = apply_rope(kpe[:, :, None, :], cos_m, sin_m)[:, :, 0]
        lat_k, lat_v = mla_expand(ckv, kpe, w_mla_kvb[l])
        ctx_k, ctx_v = mla_expand(cache_mla_ckv[:, l], cache_mla_kpe[:, l], w_mla_kvb[l])
        o_mla = block_attention(mla_q, jnp.concatenate([lat_k, ctx_k], axis=1), jnp.concatenate([lat_v, ctx_v], axis=1))
        o_swa = banded_window_attention(apply_rope(sw_q, cos_s, sin_s), apply_rope(sw_k, cos_s, sin_s), sw_v,
                                        cache_swa_k[:, l], cache_swa_v[:, l], swa_sink[l])
        z = z + gt1 * merge_heads(o_na, o_mla, o_swa, w_out[l])
        h = rms_norm(z, g_ffn[l]) * (1 + sc2) + sh2
        z = z + gt2 * moe(h, w_router, b_router, w_gate[l], w_up[l], w_down[l])
    y_sample = rms_norm(z, g_final)
    return (y_prompt, y_sample, new_na_k, new_na_v, new_mla_ckv, new_mla_kpe, new_swa_k, new_swa_v)


_drawn_inputs = setup_inputs


def setup_inputs(seed=0):
    import zlib

    import numpy as np

    out = dict(_drawn_inputs(seed))
    spreads = {}
    factors = {'cache_mla_kpe': 3.889, 'g_mla_q': 3.924, 'na_rpb': 8.0, 'swa_sink': 8.0}
    for name, (base, spread) in spreads.items():
        noise = np.random.default_rng([zlib.crc32(name.encode()), seed]).standard_normal(out[name].shape)
        drawn = base * np.exp(spread * noise) if base else spread * noise
        out[name] = __import__('jax').numpy.asarray(drawn.astype(out[name].dtype))
    for name, factor in factors.items():
        out[name] = (out[name] * factor).astype(out[name].dtype)
    return out
```

```python
from contextlib import ExitStack

import numpy as np

import concourse.bass as bass
from concourse import mybir

F32 = mybir.dt.float32
BF16 = mybir.dt.bfloat16
I32 = mybir.dt.int32
ALU = mybir.AluOpType
ACT = mybir.ActivationFunctionType
AX = mybir.AxisListType

P = 128
D = 1024
KT = D // P
DEPTH = 2
TP = 128
TS = 256
T = TP + TS
NT = T // P
TK = T + 128
GW = 64
GR = TS // GW
HD = 64
NAH, NWH, NWW = 4, 8, 16
MH, QR, KR, ND, RD, VD = 6, 256, 128, 64, 32, 64
QKD = ND + RD
SH, SKV = 6, 2
SWIN = 128
NE, NG, EPG, TOPK = 16, 4, 4, 2
DE = 512
EPS = 1e-6
NMOD = 6
NA_IN = 3 * NAH * HD
IN_W = NA_IN + QR + KR + RD + (SH + 2 * SKV) * HD
SCALE = HD ** -0.5
MSCALE = QKD ** -0.5
NEG = -1e30
BIG = 2048.0
TW = 2 * GW - 1
DRS = 2 * GR - 1

SLOTS = 6
CW = 4096
N_ADA, N_IN, N_OUT = 12, 4, 2
PASSES = NT
MOE_CH = 3 * NE

ADA_FIRST = [(0, c) for c in range(4)]
ADA_ATT = [(0, c) for c in range(4, N_ADA)] + [(1, c) for c in range(4)]
ADA_ROUTE = [(1, c) for c in range(4, N_ADA)]
ADA_ALL = ADA_FIRST + ADA_ATT + ADA_ROUTE
ATT_STEP = 4

STREAM = [[("in", i) for i in range(N_IN)] + [("out", i) for i in range(N_OUT)] for _ in range(DEPTH)]
STREAM[0] = ([("ada", *x) for x in ADA_FIRST] + STREAM[0][:N_IN] + [("ada", *x) for x in ADA_ATT] + STREAM[0][N_IN:]
             + [("ada", *x) for x in ADA_ROUTE])
MOE_AT = [len(x) for x in STREAM]
LAYER_AT = [0, MOE_AT[0] + MOE_CH]
assert all((a + b) % SLOTS == 0 for a, b in zip(MOE_AT, LAYER_AT)) and LAYER_AT[1] % SLOTS == 0
IN_PARTS = {2: 2, 3: 6}
NB = 6

CONST = {}
_at = 0
for _n, _w in (("ident", P), ("ones", P), ("tri", P), ("rot", P), ("rotm", QKD), ("iota", P), ("cos", TS), ("sin", TS),
               ("cosm", TS), ("sinm", TS), ("colmask", GW), ("before", 16), ("tokid", NT), ("swamask", 2 * TS)):
    CONST[_n] = (_at, _w)
    _at += _w
CONST_W = _at
KEPT_W = CONST_W - 2 * TS


def constants():
    c = np.zeros((P, CONST_W), np.float32)

    def put(name, v, rows=slice(0, P)):
        a, w = CONST[name]
        c[rows, a:a + w] = v

    i = np.arange(P)
    put("ident", np.eye(P))
    put("ones", 1.0)
    put("tri", (i[:, None] < i[None, :]))
    sw = (i // HD) * HD + (i % HD + HD // 2) % HD
    r = np.zeros((P, P))
    r[sw, i] = 1
    put("rot", r)
    r = np.zeros((QKD, QKD))
    j = np.arange(RD)
    r[ND + (j + RD // 2) % RD, ND + j] = 1
    put("rotm", r, slice(0, QKD))
    put("iota", i[None, :])
    t = np.arange(TS)
    row, col = (t // GW).astype(np.float32), (t % GW).astype(np.float32)

    def angles(rot):
        per = rot // 2
        inv = (np.float32(10000.0) ** (-np.arange(0, per, 2, dtype=np.float32) / np.float32(per))).astype(np.float32)
        return np.concatenate([row[:, None] * inv, col[:, None] * inv], axis=-1).astype(np.float32)

    a = angles(HD)
    cs, sn = np.cos(a).T, np.sin(a).T
    put("cos", np.concatenate([cs, cs, cs, cs]))
    put("sin", np.concatenate([-sn, sn, -sn, sn]))
    a = angles(RD)
    cs, sn = np.cos(a).T, np.sin(a).T
    put("cosm", np.concatenate([cs, cs]), slice(ND, QKD))
    put("sinm", np.concatenate([-sn, sn]), slice(ND, QKD))
    q = np.arange(GW)
    start = np.clip(q - NWW // 2, 0, GW - NWW)
    ok = (q[None, :] >= start[:, None]) & (q[None, :] < start[:, None] + NWW)
    put("colmask", np.where(np.concatenate([ok, ok]), 0.0, NEG))
    qp = np.arange(P)
    kp = np.arange(TS)
    put("swamask", np.concatenate([np.where(np.abs(kp[None, :] - (qt * P + qp[:, None])) <= SWIN, 0.0, NEG)
                                   for qt in range(2)], axis=1))
    e = np.arange(EPG)
    put("before", np.tile((e[None, :] < e[:, None]).astype(np.float32).reshape(1, 16), (P, 1)))
    put("tokid", i[:, None] + P * np.arange(NT)[None, :] - BIG)
    return c


def ada_jobs(chunks):
    rows, turned = [f"A{x}{c}" for x, c in chunks], [f"B{x}{c}" for x, c in chunks]
    return [rows[0]] + [j for pair in zip(rows[1:] + [None], turned) for j in pair if j]


def ada_in_step(i):
    k, r = divmod(i, ATT_STEP)
    if k >= len(ADA_ATT) or r not in (0, ATT_STEP // 2):
        return []
    x, c = ADA_ATT[k]
    return [f"{'B' if r else 'A'}{x}{c}"]


def job_order():
    order = ["vecA", "vecB"] + [f"x{t}{h}" for t in range(NT) for h in range(2)]
    for l in range(DEPTH):
        n = (ada_jobs(ADA_FIRST) if l == 0 else []) + ["n1c", "n1b"]
        n += ["naq0", "naq1", "nak0", "nak1"] + [f"nav{t}" for t in range(NT)] + ["cq0", "cq1"]
        n += ["ckv", "kpe", "swk"] + [f"swv{t}" for t in range(NT)] + ["swq0", "swq1", "swq2"]
        n += ["cache1", "cache2", "nqc", "nkc", "nqb", "nkb", "rk", "rkp"]
        n += ["rq0", "rq1", "rq2"] + ["rows1", "rows2"]
        n += [f"mq{h}" for h in range(MH)] + [f"mk{h}" for h in range(MH)] + ["rm0", "rm1", "rm2"]
        n += [f"mv{t}" for t in range(4)]
        for i in range(len(UNITS) + LAG_PV):
            if i < len(UNITS):
                n.append(f"S{i}")
            if 0 <= i - LAG_T < len(UNITS):
                n.append(f"T{i - LAG_T}")
            if l == 0:
                n += ada_in_step(i)
        n += [f"op{k}" for k in range(KT)]
        r = ada_jobs(ADA_ROUTE) if l == 0 else []
        n += r[0:1] + ["n2c"] + r[1:3] + ["n2b", "router"] + [f"hr{t}{h}" for t in range(NT) for h in range(2)]
        n += r[3:6] + ["rank"] + r[6:] + [f"y{t}{h}" for t in range(NT) for h in range(2)]
        order += [(l, j) for j in n]
    order += ["nfc", "nfb"] + [f"fo{t}{h}" for t in range(NT) for h in range(2)]
    return {j: k for k, j in enumerate(order)}


UNITS = []
for _pair in range(8):
    for _t in range(NT):
        for _s in range(2):
            _g, _h = (("na", 2 * _pair + _s) if _pair < 2 else ("mla", 2 * (_pair - 2) + _s) if _pair < 5
                      else ("swa", 2 * (_pair - 5) + _s))
            UNITS.append((_pair, _s, _g, _h, _t))
NU = len(UNITS)
LAG_T = 2
LAG_PV = 3
JOB = job_order()


def build(nc, A, C_dram, O):
    with ExitStack() as ctx:
        def sb(name, shape, dt=F32):
            return ctx.enter_context(nc.sbuf_tensor(name, shape, dt))

        def sem(name):
            return ctx.enter_context(nc.semaphore(name))

        ring = sb("ring", [P, SLOTS, CW])
        cst = sb("cst", [P, KEPT_W])
        zT = sb("zT", [P, KT, T])
        hT = sb("hT", [P, KT, T])
        vT = sb("vT", [P, 2, P])
        modT = sb("modT", [P, DEPTH, 48, 2])
        gain = sb("gain", [P, 2, KT, 2])
        sil = sb("sil", [P, 4, 16])
        arow = sb("arow", [2, 512])
        identb = sb("identb", [P, P], BF16)
        swab = sb("swab", [P, 2 * TS], BF16)
        sinks = sb("sinks", [P, DEPTH, 16])
        ns = sb("ns", [P, 6, NT])
        diag = sb("diag", [P, NT, P])
        st = sb("st", [P, 8, 6])
        wr = sb("wr", [P, KT, NE])
        brt = sb("brt", [P, NE])
        cnt = sb("cnt", [P, 4])
        cnti = sb("cnti", [P, 2], I32)
        idxg = sb("idxg", [P, NE + 1], I32)
        idxs = sb("idxs", [P, NE + 1], I32)
        gsl = sb("gsl", [P, NE])
        gcol = sb("gcol", [P, 2])
        wqb = sb("wqb", [P, 2, MH * QKD])
        wkvb = sb("wkvb", [P, MH * (ND + VD)])
        WORK = 16384
        work = sb("work", [P, WORK])

        at = [0]

        def carve(n, base=None):
            if base is not None:
                at[0] = base
            a = at[0]
            at[0] += n
            assert at[0] <= WORK, at[0]
            return work[:, a:a + n]

        def c3(v, a):
            return v.rearrange("p (a b) -> p a b", a=a)

        xrows = c3(carve(NT * D, 0), NT)
        vecs = c3(carve(2 * P), 2)
        swaf = carve(2 * TS)
        qna = c3(carve(2 * T, 0), 2)
        kna = c3(carve(2 * TK), 2)
        vna = c3(carve(4 * NAH * HD), 4)
        kpeT = carve(TK)
        mq = c3(carve(MH * T), MH)
        mk = c3(carve(MH * TK), MH)
        mv = c3(carve(4 * MH * VD), 4)
        swq = c3(carve(3 * T), 3)
        swk = carve(TK)
        swv = c3(carve(4 * SKV * HD), 4)
        bm_at = at[0]
        bm = c3(carve(2 * NAH * TS), 2 * NAH)
        pr_at = at[0]
        pr = c3(carve(3 * T), 3)
        pt = c3(carve(2 * T), 2)
        cnk = carve(NAH * HD, bm_at)
        cck = carve(KR)
        csk = carve(SKV * HD)
        ckp = carve(QKD)
        rows_o = carve(4 * P + RD)
        cq = c3(carve(2 * T, pr_at), 2)
        ropet = c3(carve(2 * TS), 2)
        ckvT = carve(TK)
        sqm = hT
        grow = c3(carve(2 * D, 0), 2)
        xs = carve(2 * D).rearrange("p (b k s) -> p b k s", b=2, k=KT)
        ysb = c3(carve(2 * D), 2)
        sg = carve(DE)
        am = carve(DE)
        aTs = c3(carve(DE), 4)
        yl_at = at[0]
        onehot = carve(2 * NT * EPG * P).rearrange("p (b t e s) -> p b t e s", b=2, t=NT, e=EPG)
        hrow = c3(carve(NT * D), NT)
        rw = c3(carve(12 * 48), 12)
        vals = carve(NT * NE * 3).rearrange("p (t e c) -> p t e c", t=NT, e=NE)
        cmp1 = carve(192).rearrange("p (g j i) -> p g j i", j=4, i=4)
        cmp2 = carve(192).rearrange("p (g j i) -> p g j i", j=4, i=4)
        yl = carve(2 * NT * D, yl_at).rearrange("p (t k d) -> p t k d", t=NT, k=2)

        def cv(name):
            a, w = CONST[name]
            return cst[:, a:a + w]

        ident, ones = cv("ident"), cv("ones")

        hscr = nc.dram_tensor("hscr", [T, D], F32, kind="Internal").ap()
        yscr = nc.dram_tensor("yscr", [TOPK * T, D], F32, kind="Internal").ap()
        bscr = nc.dram_tensor("bscr", [DEPTH * NAH * DRS, GW * TW], F32, kind="Internal").ap()
        bpad = sb("bpad", [P, TW])

        banks = [ctx.enter_context(nc.psum_tensor(f"bank{b}", [P, 512], F32)) for b in range(8)]
        bO = banks[6:8]
        bX, bG, bU, bA, bY = banks[0:2], banks[2], banks[3], banks[4], banks[5:7]

        s_const = sem("s_const")
        s_vec = sem("s_vec")
        s_swaf = sem("s_swaf")
        s_x = [sem(f"s_x{i}") for i in range(3)]
        s_chainv = sem("s_chainv")
        s_chaina = sem("s_chaina")
        s_chainp = sem("s_chainp")
        s_silx = sem("s_silx")
        s_sil = sem("s_sil")
        s_sq = sem("s_sq")
        s_diag = sem("s_diag")
        s_xn = sem("s_xn")
        s_hv = sem("s_hv")
        s_ha = sem("s_ha")
        s_cache = sem("s_cache")
        s_lat = sem("s_lat")
        s_bs = sem("s_bs")
        s_bp = sem("s_bp")
        s_bscr = sem("s_bscr")
        s_bmd = sem("s_bmd")
        s_bm = sem("s_bm")
        s_sqm = sem("s_sqm")
        s_kr = sem("s_kr")
        s_qkv = sem("s_qkv")
        s_kpr = sem("s_kpr")
        s_store = sem("s_store")
        s_max = sem("s_max")
        s_snk = sem("s_snk")
        s_nrm = sem("s_nrm")
        s_pv = sem("s_pv")
        s_o = sem("s_o")
        s_hscr = sem("s_hscr")
        s_mask = sem("s_mask")
        s_cnt = sem("s_cnt")
        s_oneh = sem("s_oneh")
        s_onehu = sem("s_onehu")
        s_slotp = sem("s_slotp")
        s_slot = sem("s_slot")
        s_gcol = sem("s_gcol")
        s_rest = sem("s_rest")
        s_g = [sem(f"s_g{i}") for i in range(2)]
        s_xt = sem("s_xt")
        s_xs = sem("s_xs")
        s_gd = sem("s_gd")
        s_gu = sem("s_gu")
        s_sg = sem("s_sg")
        s_a = sem("s_a")
        s_at = sem("s_at")
        s_as = sem("s_as")
        s_y = sem("s_y")
        s_ysv = sem("s_ysv")
        s_ysa = sem("s_ysa")
        s_sc = [sem(f"s_sc{i}") for i in range(2)]
        s_yl = [sem(f"s_yl{i}") for i in range(3)]
        s_ysum = sem("s_ysum")
        s_out = sem("s_out")
        s_gf = {(l, p): [sem(f"s_g_{l}{p}{i}") for i in range(2)] for l in range(DEPTH) for p in range(1, PASSES)}
        s_scf = {(l, p): [sem(f"s_sc_{l}{p}{i}") for i in range(2)] for l in range(DEPTH) for p in range(1, PASSES)}
        s_further = sem("s_further")
        s_land = [sem(f"s_land{i}") for i in range(SLOTS)]
        s_land2 = [sem(f"s_landf{i}") for i in range(SLOTS)]
        s_fill = [sem(f"s_fill{b}") for b in range(NB)]
        s_evac = [sem(f"s_evac{b}") for b in range(NB)]

        def wait(eng, s, v):
            if isinstance(v, int) and v <= 0:
                return
            eng.wait_ge(s, v)

        def bank(j):
            return banks[JOB[j] % NB]

        def fill_begin(j):
            wait(nc.tensor, s_evac[JOB[j] % NB], JOB[j] // NB)
            return bank(j)

        def filled(j, ins):
            ins.then_inc(s_fill[JOB[j] % NB], 1)

        def take(eng, j):
            eng.wait_ge(s_fill[JOB[j] % NB], JOB[j] // NB + 1)
            return bank(j)

        def evac(j, ins):
            ins.then_inc(s_evac[JOB[j] % NB], 1)

        def is_filled(eng, j):
            eng.wait_ge(s_fill[JOB[j] % NB], JOB[j] // NB + 1)

        def read_out(eng, j):
            eng.wait_ge(s_evac[JOB[j] % NB], JOB[j] // NB + 1)

        class Chain:

            def __init__(self, eng, s):
                self.eng, self.s, self.n = eng, s, 0

            def __call__(self, ins):
                self.n += 1
                ins.then_inc(self.s, 1)
                self.eng.wait_ge(self.s, self.n)

        def landed(l, k):
            slot, n = k % SLOTS, LAYER_AT[l] + k
            more = sum(parts - 1 for l2 in range(l + 1) for i, parts in IN_PARTS.items()
                       for at_ in [STREAM[l2].index(("in", i))] if at_ % SLOTS == slot and LAYER_AT[l2] + at_ <= n)
            return slot, 16 * (n // SLOTS + 1 + more)

        def arrived(eng, l, name):
            slot, v = landed(l, STREAM[l].index(name))
            eng.wait_ge(s_land[slot], v)
            return ring[:, slot, :]

        def sel(cond):
            return slice(TP, T) if cond == 0 else slice(0, TP)

        block = ctx.enter_context(nc.Block())

        def place(e_half, kind):
            pos = 3 * (1 + e_half) - 1 + kind
            return pos % SLOTS, pos // SLOTS

        def moe_land(l, p, slot, use):
            if p == 0:
                return s_land[slot], landed(l, MOE_AT[l] + SLOTS * use + slot)[1]
            return s_land2[slot], 16 * ((MOE_CH // SLOTS) * ((PASSES - 1) * l + p - 1) + use + 1)

        G_PASS = (16 * (NE // 2 + 1), 16 * (NE // 2))
        SC_PASS = 16 * (NE // 2)

        def gathers(l, p):
            return (s_g, [l * k for k in G_PASS]) if p == 0 else (s_gf[l, p], [0, 0])

        def scatters(l, p):
            return (s_sc, l * SC_PASS) if p == 0 else (s_scf[l, p], 0)

        def last_reader(l, k):
            kind, *x = STREAM[l][k]
            if kind == "ada":
                return (l, f"A{x[0]}{x[1]}")
            return (l, {"in": ("nak1", "cq1", "swv2", "swq2"), "out": ("op3", "op7")}[kind][x[0]])

        def ring_after_experts(sp, slot, n):
            s, back = ((s_gu, 1), (s_y, 2), (s_gd, 0), (s_gu, 0), (s_y, 1), (s_y, 0))[slot]
            sp.wait_ge(s, n * NE - back)

        wg_d = A["w_gate"].rearrange("l e (p k) n -> l e p (k n)", p=P)
        wu_d = A["w_up"].rearrange("l e (p k) n -> l e p (k n)", p=P)
        wd_d = A["w_down"].rearrange("l e (p k) n -> l e p (k n)", p=P)

        @block.sync
        def _(sp):
            sp.dma_start(cst[:], C_dram[:, 0:KEPT_W]).then_inc(s_const, 16)
            row = 0
            for name, n in (("b_ada", DEPTH * 48), ("g_attn", DEPTH * KT), ("g_ffn", DEPTH * KT)):
                sp.dma_start(vecs[row:row + n, 0, :], A[name].rearrange("l (j p) -> (l j) p", p=P)).then_inc(s_vec, 16)
                row += n
            sp.dma_start(vecs[0:8, 1, :], A["c"].rearrange("o (j p) -> (o j) p", p=P)).then_inc(s_vec, 16)
            sp.dma_start(vecs[8:16, 1, :], A["c_ctx"].rearrange("(j p) -> j p", p=P)).then_inc(s_vec, 16)
            sp.dma_start(vecs[16:24, 1, :], A["g_final"].rearrange("(j p) -> j p", p=P)).then_inc(s_vec, 16)
            sp.dma_start(vecs[24:28, 1, :], A["g_mla_q"].rearrange("l (j p) -> (l j) p", p=P)).then_inc(s_vec, 16)
            sp.dma_start(vecs[28:30, 1, :], A["g_mla_kv"]).then_inc(s_vec, 16)
            for t in range(NT):
                src = A["x_prompt"][0] if t == 0 else A["x_sample"][0, (t - 1) * P:t * P, :]
                sp.dma_start(xrows[:, t, :], src).then_inc(s_x[t], 16)

            def chunk(l, k, parts):
                slot = k % SLOTS
                if k >= SLOTS:
                    is_filled(sp, last_reader(l, k - SLOTS))
                elif l > 0:
                    ring_after_experts(sp, slot, PASSES * (l - 1) + 1)
                for dst, src in parts(ring[:, slot, :]):
                    sp.dma_start(dst, src).then_inc(s_land[slot], 16)

            def cols(w, c, n):
                def parts(r):
                    return [(r[:, 0:KT * n].rearrange("p (k n) -> p k n", k=KT),
                             w.rearrange("(k p) n -> p k n", p=P)[:, :, c:c + n])]
                return parts

            def in_tail(l):
                w = A["w_in"][l].rearrange("(k p) n -> p k n", p=P)
                a = NA_IN + QR
                b = a + KR + RD + SH * HD

                def parts(r):
                    v = r[:, 0:KT * 416].rearrange("p (k n) -> p k n", k=KT)
                    return [(v[:, :, 0:KR + RD], w[:, :, a:a + KR + RD]), (v[:, :, KR + RD:416], w[:, :, b:b + 256])]
                return parts

            def in_swq(l):
                w = A["w_in"][l].rearrange("(k p) n -> p k n", p=P)
                a = NA_IN + QR + KR + RD

                def parts(r):
                    v = r[:, 0:KT * 384].rearrange("p (k h s d) -> p k h s d", k=KT, h=3, s=2)
                    return [(v[:, :, h, s, :], w[:, :, a + (3 * s + h) * HD:a + (3 * s + h + 1) * HD])
                            for h in range(3) for s in range(2)]
                return parts

            for l in range(DEPTH):
                w_in = (cols(A["w_in"][l], 0, 512), cols(A["w_in"][l], 512, 512), in_tail(l), in_swq(l))
                for k, (kind, *x) in enumerate(STREAM[l]):
                    if kind == "ada":
                        chunk(l, k, cols(A["w_ada"][x[0]], x[1] * 512, 512))
                    elif kind == "in":
                        chunk(l, k, w_in[x[0]])
                    else:
                        chunk(l, k, cols(A["w_out"][l], x[0] * 512, 512))

                def load(l, p, slot, use, w, e):
                    src = w[l, e] if isinstance(e, int) else w[l, bass.ds(e, 1)].rearrange("a p n -> (a p) n")
                    sp.dma_start(ring[:, slot, :], src).then_inc(moe_land(l, p, slot, 0)[0], 16)

                def stream(p):
                    n = PASSES * l + p

                    def before(slot):
                        if p == 0:
                            is_filled(sp, last_reader(l, MOE_AT[l] - SLOTS + slot))
                        else:
                            ring_after_experts(sp, slot, n)
                    before(0)
                    load(l, p, 0, 0, wg_d, 0)
                    before(1)
                    load(l, p, 1, 0, wu_d, 0)

                    def step(i, u):
                        e = 2 * i + 1 + u
                        for kind, (w, s, back) in enumerate(((wg_d, s_gd, 1), (wu_d, s_gu, 1), (wd_d, s_y, 2))):
                            slot, use = place(u, kind)
                            if isinstance(i, int) and i == 0 and use == 0:
                                before(slot)
                            elif isinstance(i, int) and i == 0:
                                sp.wait_ge((s_gd, s_gu)[slot], n * NE + 1)
                            else:
                                sp.wait_ge(s, e + n * NE - back)
                            load(l, p, slot, use, w, e - (kind == 2))
                    step(0, 0)
                    step(0, 1)
                    with sp.Fori(1, NE // 2 - 1) as i:
                        step(i, 0)
                        step(i, 1)
                    step(NE // 2 - 1, 0)
                    sp.wait_ge(s_gd, n * NE + NE - 1)
                    load(l, p, 5, 0, wd_d, NE - 1)
                    if p:
                        sp.wait_ge(s_y, (n + 1) * NE)

                stream(0)
                sp.wait_ge(s_cnt, l + 1)
                most = sp.value_load(cnti[0:1, 0:1], min_val=0, max_val=T)
                for p in range(1, PASSES):
                    with sp.If(most > P * p):
                        stream(p)
                    with sp.Else():
                        for slot, s in enumerate(s_land2):
                            before_n = (PASSES - 1) * l + p - 1
                            wait(sp, s, 16 * (MOE_CH // SLOTS) * before_n)
                            sp.sem_inc(s, 16 * MOE_CH // SLOTS)

            for t in range(NT):
                read_out(sp, f"fo{t}0")
                read_out(sp, f"fo{t}1")
                dst = O["y_prompt"][0] if t == 0 else O["y_sample"][0, (t - 1) * P:t * P, :]
                sp.dma_start(dst, xrows[:, t, :]).then_inc(s_out, 16)
            sp.wait_ge(s_out, 16 * NT)
            sp.wait_ge(s_store, 16 * 6 * DEPTH)

        @block.tensor
        def _(pe):
            mm = nc.tensor.matmul
            turn_ = nc.tensor.transpose

            def turn4(j, src):
                b = fill_begin(j)
                for k in range(4):
                    last = turn_(b[:, k * P:(k + 1) * P], src(k), ident)
                filled(j, last)

            def sums(j, sq, nk):
                b = fill_begin(j)
                for t in range(NT):
                    for k in range(nk):
                        last = mm(b[:, t:t + 1], sq[:, k, t * P:(t + 1) * P], ones[:, 0:1], start=(k == 0), stop=(k == nk - 1))
                filled(j, last)

            def spread(j, n):
                pe.wait_ge(s_diag, n)
                b = fill_begin(j)
                filled(j, mm(b[:, 0:T], ones, diag[:].rearrange("p t q -> p (t q)"), start=True, stop=True))

            pe.wait_ge(s_const, 16)
            pe.wait_ge(s_vec, 16 * 8)
            b = fill_begin("vecA")
            filled("vecA", turn_(b[:, 0:P], vecs[:, 0, :], ident))
            b = fill_begin("vecB")
            filled("vecB", turn_(b[:, 0:30], vecs[0:30, 1, :], ident[0:30, 0:30]))
            for t in range(NT):
                pe.wait_ge(s_x[t], 16)
                for h in range(2):
                    turn4(f"x{t}{h}", lambda k: xrows[:, t, (4 * h + k) * P:(4 * h + k + 1) * P])
            pe.wait_ge(s_sil, 1)

            for l in range(DEPTH):
                def ada(j):
                    kind, x, c = j[0], int(j[1]), int(j[2:])
                    if kind == "A":
                        w = arrived(pe, l, ("ada", x, c)).rearrange("p (k n) -> p k n", k=KT)
                        b = fill_begin((l, j))
                        for k in range(KT):
                            last = mm(b[0:2, :], sil[:, 3, k::KT], w[:, k, :], start=(k == 0), stop=(k == KT - 1))
                    else:
                        read_out(pe, (l, f"A{x}{c}"))
                        b = fill_begin((l, j))
                        for k in range(4):
                            last = turn_(b[:, 2 * k:2 * k + 2], arow[0:2, k * P:(k + 1) * P], ident[0:2, 0:2])
                    filled((l, j), last)

                route = ada_jobs(ADA_ROUTE) if l == 0 else []

                def proj(name, w, c, m):
                    b = fill_begin((l, name))
                    for k in range(KT):
                        last = mm(b[0:m, 0:T], w[:, k, c:c + m], hT[:, k, :], start=(k == 0), stop=(k == KT - 1))
                    filled((l, name), last)

                def proj_rows(name, w, c, m, t):
                    b = fill_begin((l, name))
                    for k in range(KT):
                        last = mm(b[:, 0:m], hT[:, k, t * P:(t + 1) * P], w[:, k, c:c + m], start=(k == 0), stop=(k == KT - 1))
                    filled((l, name), last)

                for j in ada_jobs(ADA_FIRST) if l == 0 else []:
                    ada(j)
                pe.wait_ge(s_sq, 2 * l + 1)
                sums((l, "n1c"), hT, KT)
                spread((l, "n1b"), 4 * l + 1)
                pe.wait_ge(s_hv, 2 * l + 1)
                pe.wait_ge(s_ha, 2 * l + 1)
                w = arrived(pe, l, ("in", 0)).rearrange("p (k n) -> p k n", k=KT)
                for i, name in enumerate(("naq0", "naq1", "nak0", "nak1")):
                    proj(name, w, i * P, P)
                w = arrived(pe, l, ("in", 1)).rearrange("p (k n) -> p k n", k=KT)
                for t in range(NT):
                    proj_rows(f"nav{t}", w, 0, NAH * HD, t)
                for i in range(2):
                    proj(f"cq{i}", w, NAH * HD + i * P, P)
                w = arrived(pe, l, ("in", 2))[:, 0:KT * 416].rearrange("p (k n) -> p k n", k=KT)
                proj("ckv", w, 0, KR)
                proj("kpe", w, KR - ND, QKD)
                proj("swk", w, KR + RD, P)
                for t in range(NT):
                    proj_rows(f"swv{t}", w, KR + RD + P, P, t)
                w = arrived(pe, l, ("in", 3))[:, 0:KT * 384].rearrange("p (k n) -> p k n", k=KT)
                for i in range(3):
                    proj(f"swq{i}", w, i * P, P)
                pe.wait_ge(s_cache, 16 * 6 * (l + 1))
                turn4((l, "cache1"), lambda k: (cnk[:, 0:P], cnk[:, P:2 * P], cck, csk)[k])
                b = fill_begin((l, "cache2"))
                filled((l, "cache2"), turn_(b[0:QKD, 0:P], ckp, ident))
                pe.wait_ge(s_sqm, l + 1)
                sums((l, "nqc"), sqm[:, 0:2, :], 2)
                sums((l, "nkc"), sqm[:, 2:3, :], 1)
                spread((l, "nqb"), 4 * l + 2)
                spread((l, "nkb"), 4 * l + 3)
                read_out(pe, (l, "swk"))
                b = fill_begin((l, "rk"))
                filled((l, "rk"), mm(b[:, 0:TS], cv("rot"), swk[:, TP:T], start=True, stop=True))
                read_out(pe, (l, "kpe"))
                b = fill_begin((l, "rkp"))
                filled((l, "rkp"), mm(b[0:QKD, 0:TS], cv("rotm")[0:QKD, :], kpeT[0:QKD, TP:T], start=True, stop=True))
                read_out(pe, (l, "swq2"))
                for i in range(3):
                    b = fill_begin((l, f"rq{i}"))
                    filled((l, f"rq{i}"), mm(b[:, 0:TS], cv("rot"), swq[:, i, TP:T], start=True, stop=True))
                read_out(pe, (l, "nkb"))
                turn4((l, "rows1"), lambda k: (kna[:, 0, 0:P], kna[:, 1, 0:P], ckvT[:, 0:P], swk[:, 0:P])[k])
                b = fill_begin((l, "rows2"))
                filled((l, "rows2"), turn_(b[:, 0:QKD], kpeT[0:QKD, 0:P], ident[0:QKD, 0:QKD]))
                pe.wait_ge(s_lat, 16 * 2 * (l + 1))
                read_out(pe, (l, "cache1"))
                for h in range(MH):
                    b = fill_begin((l, f"mq{h}"))
                    for k in range(2):
                        last = mm(b[0:QKD, 0:T], wqb[:, k, h * QKD:(h + 1) * QKD], cq[:, k, :], start=(k == 0), stop=(k == 1))
                    filled((l, f"mq{h}"), last)
                for h in range(MH):
                    b = fill_begin((l, f"mk{h}"))
                    filled((l, f"mk{h}"), mm(b[0:ND, :], wkvb[:, h * P:h * P + ND], ckvT, start=True, stop=True))
                for i in range(3):
                    read_out(pe, (l, f"mq{2 * i + 1}"))
                    b = fill_begin((l, f"rm{i}"))
                    filled((l, f"rm{i}"), mm(b[0:QKD, :], cv("rotm")[0:QKD, :],
                                             mq[0:QKD, 2 * i:2 * i + 2, TP:T], start=True, stop=True))
                vcols = wkvb[:].rearrange("p (h c) -> p h c", h=MH)[:, :, ND:]
                for t in range(4):
                    b = fill_begin((l, f"mv{t}"))
                    filled((l, f"mv{t}"), mm(b[:, 0:MH * VD], ckvT[:, t * P:(t + 1) * P], vcols, start=True, stop=True))

                pe.wait_ge(s_qkv, l + 1)
                read_out(pe, (l, "mv3"))
                pe.wait_ge(s_kpr, l + 1)
                pe.wait_ge(s_bm, l + 1)

                def scores(u):
                    pair, s, g, h, t = UNITS[u]
                    q = slice(t * P, (t + 1) * P)
                    ks = slice(0, TP) if t == 0 else slice(TP, TK)
                    n = ks.stop - ks.start
                    b = fill_begin((l, f"S{u}"))
                    if g == "na":
                        r = slice(64 * (h % 2), 64 * (h % 2) + 64)
                        lhs, rhs = qna[r, h // 2, q], kna[r, h // 2, ks]
                    elif g == "mla":
                        lhs, rhs = mq[0:QKD, h, q], mk[0:QKD, h, ks]
                    else:
                        r = slice(64 * (h // 3), 64 * (h // 3) + 64)
                        lhs, rhs = swq[r, h % 3, q], swk[r, ks]
                    masked = t > 0 and g != "mla"
                    last = mm(b[:, 0:n], lhs, rhs, start=True, stop=True)
                    if masked and g == "na":
                        last = mm(b[:, 0:TS], ident, bm[:, (t - 1) * NAH + h, :], start=False, stop=True, skip_group_check=True)
                    elif masked:
                        last = mm(b[:, 0:TS], identb[:], swab[:, (t - 1) * TS:t * TS], start=False, stop=True, skip_group_check=True)
                    filled((l, f"S{u}"), last)

                def turn(u):
                    pe.wait_ge(s_nrm, l * NU + u + 1)
                    b = fill_begin((l, f"T{u}"))
                    for c in range(1 if UNITS[u][4] == 0 else 3):
                        last = turn_(b[:, c * P:(c + 1) * P], pr[:, u % 3, c * P:(c + 1) * P], ident)
                    filled((l, f"T{u}"), last)

                def values(u):
                    pair, s, g, h, t = UNITS[u]
                    read_out(pe, (l, f"T{u}"))
                    if t == 0 and s == 0:
                        wait(pe, s_o, l * 8 + pair - 1)
                    o = bO[pair % 2][64 * s:64 * s + 64, t * P:(t + 1) * P]
                    chunks = (0,) if t == 0 else (1, 2, 3)
                    for i, c in enumerate(chunks):
                        v = (vna[:, c, h * HD:(h + 1) * HD] if g == "na" else mv[:, c, h * VD:(h + 1) * VD] if g == "mla"
                             else swv[:, c, (h // 3) * HD:(h // 3 + 1) * HD])
                        last = mm(o, v, pt[:, u % 2, i * P:(i + 1) * P], start=(i == 0), stop=(i == len(chunks) - 1))
                    last.then_inc(s_pv, 1)

                for i in range(NU + LAG_PV):
                    if i < NU:
                        scores(i)
                    if 0 <= i - LAG_T < NU:
                        turn(i - LAG_T)
                    for j in ada_in_step(i) if l == 0 else []:
                        ada(j)
                    if i >= LAG_PV:
                        values(i - LAG_PV)

                pe.wait_ge(s_o, 8 * (l + 1))
                for n in range(KT):
                    if n % 4 == 0:
                        w = arrived(pe, l, ("out", n // 4)).rearrange("p (k n) -> p k n", k=KT)
                    proj(f"op{n}", w, (n % 4) * P, P)
                for j in route[0:1]:
                    ada(j)
                pe.wait_ge(s_sq, 2 * l + 2)
                sums((l, "n2c"), hT, KT)
                for j in route[1:3]:
                    ada(j)
                spread((l, "n2b"), 4 * l + 4)
                pe.wait_ge(s_hv, 2 * l + 2)
                pe.wait_ge(s_ha, 2 * l + 2)
                if l == 0:
                    pe.wait_ge(s_bs, 16 * 4)
                b = fill_begin((l, "router"))
                for t in range(NT):
                    for k in range(KT):
                        last = mm(b[:, t * NE:(t + 1) * NE], hT[:, k, t * P:(t + 1) * P], wr[:, k, :],
                                  start=(k == 0), stop=(k == KT - 1))
                filled((l, "router"), last)
                for t in range(NT):
                    for h in range(2):
                        turn4((l, f"hr{t}{h}"), lambda k: hT[:, 4 * h + k, t * P:(t + 1) * P])
                for j in route[3:6]:
                    ada(j)
                pe.wait_ge(s_mask, l + 1)
                m = rw[:, 4, :].rearrange("p (t e) -> p t e", t=NT)
                b = fill_begin((l, "rank"))
                for t in range(NT):
                    for t2 in range(t):
                        mm(b[:, t * NE:(t + 1) * NE], ones, m[:, t2, :], start=(t2 == 0), stop=False)
                    mm(b[:, t * NE:(t + 1) * NE], cv("tri"), m[:, t, :], start=(t == 0), stop=True)
                for t in range(NT):
                    last = mm(b[:, 3 * NE:4 * NE], ones, m[:, t, :], start=(t == 0), stop=(t == NT - 1))
                filled((l, "rank"), last)
                for j in route[6:]:
                    ada(j)
                for bk in range(NB):
                    done = max(n for n in range(JOB[(l, "y00")]) if n % NB == bk)
                    pe.wait_ge(s_evac[bk], done // NB + 1)

                def experts(p):
                    n = PASSES * l + p
                    for q in range(NG):
                        pe.wait_ge(s_oneh, n * NG + q + 1)
                        for t in range(NT):
                            for e in range(EPG):
                                c = (q * EPG + e) * 3
                                last = mm(bA[:, c:c + 3], onehot[:, q % 2, t, e, :], vals[:, t, q * EPG + e, :],
                                          start=(q == 0 and t == 0 and e == 0), stop=(t == NT - 1), skip_group_check=True)
                        last.then_inc(s_onehu if q < NG - 1 else s_slotp, 1)

                    def tokens(e, par, land):
                        pe.wait_ge(gathers(l, p)[0][par], land)
                        wait(pe, s_xs, n * (NE + 1) + e)
                        for k in range(KT):
                            last = turn_(bX[k // 4][:, (k % 4) * P:(k % 4 + 1) * P], grow[:, par, k::KT], ident)
                        last.then_inc(s_xt, 1)

                    def product(b, par, land, done):
                        pe.wait_ge(*land)
                        w = ring[:, land_slot(land[0]), :].rearrange("p (k n) -> p k n", k=KT)
                        for k in range(KT):
                            last = mm(b[:], xs[:, par, k, :], w[:, k, :], start=(k == 0), stop=(k == KT - 1))
                        last.then_inc(done, 1)

                    def gate_up(e, par, gate, up):
                        pe.wait_ge(s_xs, n * (NE + 1) + e + 1)
                        wait(pe, s_a, n * NE + e)
                        product(bG, par, gate, s_gd)
                        product(bU, par, up, s_gu)

                    def down(e, land):
                        pe.wait_ge(s_as, n * NE + e + 1)
                        wait(pe, s_ysv, n * NE + e)
                        wait(pe, s_ysa, n * NE + e)
                        pe.wait_ge(*land)
                        w = ring[:, land_slot(land[0]), :].rearrange("p (k n) -> p k n", k=4)
                        for half in range(2):
                            for k in range(4):
                                last = mm(bY[half][:], aTs[:, k, :], w[:, k, half * 512:(half + 1) * 512],
                                          start=(k == 0), stop=(k == 3))
                        last.then_inc(s_y, 1)

                    def turn_a(e):
                        pe.wait_ge(s_a, n * NE + e + 1)
                        for k in range(4):
                            last = turn_(bA[:, k * P:(k + 1) * P], am[:, k::4], ident)
                        last.then_inc(s_at, 1)

                    def land_slot(s):
                        return (s_land if p == 0 else s_land2).index(s)

                    g0, g1 = gathers(l, p)[1]
                    tokens(0, 0, g0 + 16)
                    gate_up(0, 0, moe_land(l, p, 0, 0), moe_land(l, p, 1, 0))
                    tokens(1, 1, g1 + 16)
                    pe.wait_ge(s_slot, n + 1)
                    turn_a(0)

                    def step(i, u):
                        e = 2 * i + 1 + u
                        gate, up, dn = [(s, v + 16 * i) for s, v in (moe_land(l, p, *place(u, kind)) for kind in range(3))]
                        gate_up(e, 1 - u, gate, up)
                        tokens(e + 1, u, (g0 if u == 0 else g1) + 16 * i + 32)
                        down(e - 1, dn)
                        turn_a(e)
                    step(0, 0)
                    step(0, 1)
                    with pe.Fori(1, NE // 2 - 1) as i:
                        step(i, 0)
                        step(i, 1)
                    step(NE // 2 - 1, 0)
                    down(NE - 1, moe_land(l, p, 5, NE // 2 - 1))

                experts(0)
                pe.wait_ge(s_cnt, l + 1)
                most = pe.value_load(cnti[0:1, 0:1], min_val=0, max_val=T)
                for p in range(1, PASSES):
                    with pe.If(most > P * p):
                        experts(p)
                    with pe.Else():
                        pe.wait_ge(s_y, NE * (PASSES * l + p))
                        for s, k in ((s_onehu, NG - 1), (s_slotp, 1), (s_xt, NE + 1), (s_gd, NE), (s_gu, NE), (s_at, NE), (s_y, NE)):
                            pe.sem_inc(s, k)
                done = PASSES * (l + 1)
                pe.wait_ge(s_xs, done * (NE + 1))
                pe.wait_ge(s_as, done * NE)
                pe.wait_ge(s_ysv, done * NE)
                pe.wait_ge(s_ysa, done * NE)
                for t in range(NT):
                    pe.wait_ge(s_ysum, l * NT + t + 1)
                    for h in range(2):
                        turn4((l, f"y{t}{h}"), lambda k: yl[:, t, 0, (4 * h + k) * P:(4 * h + k + 1) * P])

            pe.wait_ge(s_sq, 2 * DEPTH + 1)
            sums("nfc", hT, KT)
            spread("nfb", 4 * DEPTH + 1)
            pe.wait_ge(s_hv, 2 * DEPTH + 1)
            for t in range(NT):
                for h in range(2):
                    turn4(f"fo{t}{h}", lambda k: hT[:, 4 * h + k, t * P:(t + 1) * P])

        @block.scalar
        def _(act):
            A_ = nc.scalar.activation
            act.wait_ge(s_silx, 1)
            A_(sil[:, 1, :], sil[:, 0, :], ACT.Exp, scale=-1.0).then_inc(s_silx, 1)

            def copy(j, dst, n, rows=slice(0, P), scale=1.0):
                b = take(act, j)
                src = b[rows, 0:n]
                if len(dst.shape) == 3:
                    src = src.rearrange("p (a b) -> p a b", a=dst.shape[1])
                evac(j, A_(dst, src, ACT.Copy, scale=scale))

            for t in range(NT):
                copy(f"x{t}1", zT[:, 4:8, t * P:(t + 1) * P], 512)

            def squares():
                for k in range(0, KT, 4):
                    last = A_(hT[:, k:k + 4, :], zT[:, k:k + 4, :], ACT.Square)
                last.then_inc(s_sq, 1)

            def modulate(l, which):
                act.wait_ge(s_xn, 2 * l + which + 1)
                for k in range(4):
                    for cond in range(2):
                        x = hT[:, k, sel(cond)]
                        last = A_(x, x, ACT.Identity, bias=modT[:, l, 24 * which + k, cond:cond + 1],
                                  scale=gain[:, which, k, cond:cond + 1])
                last.then_inc(s_ha, 1)

            def ada_row(l, j):
                if j[0] == "A":
                    before = ADA_ALL.index((int(j[1]), int(j[2:]))) - 1
                    if before >= 0:
                        is_filled(act, (l, "B{}{}".format(*ADA_ALL[before])))
                    copy((l, j), arow[0:2, :], 512, rows=slice(0, 2))

            for l in range(DEPTH):
                route = ada_jobs(ADA_ROUTE) if l == 0 else []
                if l == 0:
                    for j in ada_jobs(ADA_FIRST):
                        ada_row(l, j)
                    read_out(act, "x20")
                    read_out(act, "x21")
                else:
                    read_out(act, (l - 1, "y21"))
                squares()
                modulate(l, 0)
                for i in range(2):
                    copy((l, f"naq{i}"), qna[:, i, :], T, scale=SCALE)
                for i in range(2):
                    copy((l, f"nak{i}"), kna[:, i, 0:T], T)
                for t in range(NT):
                    copy((l, f"nav{t}"), vna[:, t, :], NAH * HD)
                copy((l, "kpe"), kpeT[0:QKD, 0:T], T, rows=slice(0, QKD))
                for t in range(NT):
                    copy((l, f"swv{t}"), swv[:, t, :], P)
                for i in range(3):
                    copy((l, f"swq{i}"), swq[:, i, :], T, scale=SCALE)
                b = take(act, (l, "cache1"))
                A_(kna[:, :, T:TK], b[:, 0:2 * P].rearrange("p (a b) -> p a b", a=2), ACT.Copy)
                A_(ckvT[:, T:TK], b[:, 2 * P:3 * P], ACT.Copy)
                evac((l, "cache1"), A_(swk[:, T:TK], b[:, 3 * P:4 * P], ACT.Copy))
                copy((l, "cache2"), kpeT[0:QKD, T:TK], P, rows=slice(0, QKD))
                copy((l, "rows1"), rows_o[:, 0:4 * P], 4 * P)
                b = take(act, (l, "rows2"))
                evac((l, "rows2"), A_(rows_o[:, 4 * P:4 * P + RD], b[:, ND:QKD], ACT.Copy))
                for h in range(MH):
                    copy((l, f"mq{h}"), mq[0:QKD, h, :], T, rows=slice(0, QKD), scale=MSCALE)
                for h in range(MH):
                    copy((l, f"mk{h}"), mk[0:ND, h, :], TK, rows=slice(0, ND))
                for t in range(4):
                    copy((l, f"mv{t}"), mv[:, t, :], MH * VD)

                def exps(u):
                    pair, s, g, h, t = UNITS[u]
                    n = P if t == 0 else T
                    r = u % 8
                    if u >= 3:
                        is_filled(act, (l, f"T{u - 3}"))
                    if u == 0:
                        is_filled(act, (l, "mv3"))
                        act.wait_ge(s_qkv, l + 1)
                    act.wait_ge(s_max, l * NU + u + 1)
                    b = take(act, (l, f"S{u}"))
                    evac((l, f"S{u}"), A_(pr[:, u % 3, 0:n], b[:, 0:n], ACT.Exp, bias=st[:, r, 1:2], accum_out=st[:, r, 2:3]))
                    if g == "swa":
                        A_(st[:, r, 3:4], sinks[:, l, 2 * pair + s:2 * pair + s + 1], ACT.Exp, bias=st[:, r, 1:2]).then_inc(s_snk, 1)

                def turned(u):
                    n = P if UNITS[u][4] == 0 else T
                    if u >= 2:
                        act.wait_ge(s_pv, l * NU + u - 1)
                    copy((l, f"T{u}"), pt[:, u % 2, 0:n], n)

                for i in range(NU + LAG_T):
                    if i < NU:
                        exps(i)
                    if i >= LAG_T:
                        turned(i - LAG_T)
                    for j in ada_in_step(i) if l == 0 else []:
                        ada_row(l, j)

                read_out(act, (l, "op7"))
                squares()
                for j in route[0:3]:
                    ada_row(l, j)
                modulate(l, 1)
                b = take(act, (l, "router"))
                evac((l, "router"), A_(rw[:, 0, :], b[:, 0:NT * NE], ACT.Exp, scale=-1.0))
                for t in range(NT):
                    copy((l, f"hr{t}0"), hrow[:, t, 0:512], 512)
                    copy((l, f"hr{t}1"), hrow[:, t, 512:1024], 512)
                    read_out(act, (l, f"hr{t}1"))
                    act.dma_start(hscr[t * P:(t + 1) * P, :], hrow[:, t, :]).then_inc(s_hscr, 16)
                for j in route[3:]:
                    ada_row(l, j)

                def experts(p):
                    n = PASSES * l + p

                    def rows_in(e, par, first=False):
                        act.wait_ge(s_xt, n * (NE + 1) + e + 1)
                        wait(act, s_gu, n * NE + e - 1 if not first else n * NE)
                        A_(xs[:, par, 0:4, :], bX[0][:].rearrange("p (k s) -> p k s", k=4), ACT.Copy)
                        A_(xs[:, par, 4:8, :], bX[1][:].rearrange("p (k s) -> p k s", k=4), ACT.Copy).then_inc(s_xs, 1)

                    def silu(e):
                        act.wait_ge(s_gu, n * NE + e + 1)
                        wait(act, s_a, n * NE + e)
                        A_(sg, bG[:], ACT.Silu).then_inc(s_sg, 1)

                    def rows_out(e, par, stored):
                        act.wait_ge(s_y, n * NE + e + 1)
                        wait(act, scatters(l, p)[0][par], stored)
                        A_(ysb[:, par, 0:512], bY[0][:], ACT.Copy).then_inc(s_ysa, 1)

                    rows_in(0, 0, True)
                    silu(0)
                    rows_in(1, 1, True)

                    def step(i, u):
                        e = 2 * i + 1 + u
                        silu(e)
                        rows_in(e + 1, u)
                        rows_out(e - 1, u, scatters(l, p)[1] + 16 * i)
                    step(0, 0)
                    step(0, 1)
                    with act.Fori(1, NE // 2 - 1) as i:
                        step(i, 0)
                        step(i, 1)
                    step(NE // 2 - 1, 0)
                    rows_out(NE - 1, 1, scatters(l, p)[1] + SC_PASS - 16)

                experts(0)
                act.wait_ge(s_cnt, l + 1)
                most = act.value_load(cnti[0:1, 0:1], min_val=0, max_val=T)
                for p in range(1, PASSES):
                    with act.If(most > P * p):
                        experts(p)
                    with act.Else():
                        act.wait_ge(s_ysa, NE * (PASSES * l + p))
                        for s, k in ((s_xs, NE + 1), (s_sg, NE), (s_ysa, NE)):
                            act.sem_inc(s, k)
                act.wait_ge(s_sc[0], (l + 1) * SC_PASS)
                act.wait_ge(s_sc[1], (l + 1) * SC_PASS)
                act.wait_ge(s_further, (PASSES - 1) * (l + 1))
                for t in range(NT):
                    for k in range(TOPK):
                        act.dma_start(yl[:, t, k, :], yscr[k * T + t * P:k * T + (t + 1) * P, :]).then_inc(s_yl[t], 16)

            read_out(act, (DEPTH - 1, "y21"))
            squares()
            for t in range(NT):
                copy(f"fo{t}0", xrows[:, t, 0:512], 512)

        @block.vector
        def _(v):
            tt, ts, stt, tc = (nc.vector.tensor_tensor, nc.vector.tensor_scalar, nc.vector.scalar_tensor_tensor,
                               nc.vector.tensor_copy)
            chain = Chain(v, s_chainv)
            v.wait_ge(s_const, 16)
            tc(identb[:], ident)
            v.wait_ge(s_swaf, 16)
            tc(swab[:], swaf)
            for name, i, n in (("vecA", 0, P), ("vecB", 1, 30)):
                b = take(v, name)
                evac(name, tc(vT[:, i, 0:n], b[:, 0:n]))
            read_out(v, "vecB")
            tc(sil[:, 0, :], vT[:, 1, 0:16]).then_inc(s_silx, 1)
            v.wait_ge(s_silx, 2)
            chain(ts(sil[:, 2, :], sil[:, 1, :], 1.0, None, ALU.add))
            chain(nc.vector.reciprocal(sil[:, 1, :], sil[:, 2, :]))
            tt(sil[:, 3, :], sil[:, 0, :], sil[:, 1, :], ALU.mult).then_inc(s_sil, 1)
            for t in range(NT):
                b = take(v, f"x{t}0")
                evac(f"x{t}0", tc(zT[:, 0:4, t * P:(t + 1) * P], b[:].rearrange("p (a b) -> p a b", a=4)))
            read_out(v, "x20")
            read_out(v, "x21")

            def rsqrt(j, nfeat):
                b = take(v, j)
                x, y, t1, t2, xh = ns[:, 0, :], ns[:, 1, :], ns[:, 2, :], ns[:, 3, :], ns[:, 5, :]
                evac(j, ts(x, b[:, 0:NT], 1.0 / nfeat, EPS, ALU.mult, ALU.add))
                read_out(v, j)
                chain(ts(ns[:, 4, :].bitcast(I32), x.bitcast(I32), 1, None, ALU.logical_shift_right))
                ts(xh, x, -0.5, None, ALU.mult)
                chain(ts(y.bitcast(I32), ns[:, 4, :].bitcast(I32), -1.0, 1597463007.0, ALU.mult, ALU.add))
                for _ in range(3):
                    chain(tt(t1, y, y, ALU.mult))
                    chain(tt(t2, t1, xh, ALU.mult))
                    chain(stt(y, t2, 1.5, y, ALU.add, ALU.mult))
                for t in range(NT):
                    ins = ts(diag[:, t, :], ident, y[:, t:t + 1], None, ALU.mult)
                ins.then_inc(s_diag, 1)

            def ada(l, j):
                if j[0] == "B":
                    x, c = int(j[1]), int(j[2:])
                    b = take(v, (l, j))
                    evac((l, j), tt(modT[:, x, 4 * c:4 * c + 4, :], b[:, 0:8].rearrange("p (j c) -> p j c", j=4),
                                    vT[:, 0, x * 48 + 4 * c:x * 48 + 4 * c + 4].unsqueeze(2).to_broadcast([P, 4, 2]), ALU.add))

            def gains(l, which):
                a = 96 + 16 * which + l * KT
                g = vT[:, 0, a:a + KT].unsqueeze(2).to_broadcast([P, KT, 2])
                chain(ts(gain[:, which], modT[:, l, 24 * which + 8:24 * which + 16, :], 1.0, None, ALU.add))
                chain(tt(gain[:, which], gain[:, which], g, ALU.mult))

            def normalise(j, l, which):
                b = take(v, j)
                half = b[:, 0:T].unsqueeze(1).to_broadcast([P, 4, T])
                ins = tt(hT[:, 0:4, :], zT[:, 0:4, :], half, ALU.mult)
                if l is not None:
                    ins.then_inc(s_xn, 1)
                evac(j, tt(hT[:, 4:8, :], zT[:, 4:8, :], half, ALU.mult))
                read_out(v, j)
                if l is None:
                    for k in range(KT):
                        ins = ts(hT[:, k, :], hT[:, k, :], vT[:, 1, 16 + k:17 + k], None, ALU.mult)
                else:
                    for k in range(4, KT):
                        for cond in range(2):
                            x = hT[:, k, sel(cond)]
                            ins = ts(x, x, gain[:, which, k, cond:cond + 1], modT[:, l, 24 * which + k, cond:cond + 1],
                                     ALU.mult, ALU.add)
                ins.then_inc(s_hv, 1)

            for l in range(DEPTH):
                route = ada_jobs(ADA_ROUTE) if l == 0 else []
                if l == 0:
                    for j in ada_jobs(ADA_FIRST):
                        ada(l, j)
                read_out(v, (0, "B{}{}".format(*(ADA_FIRST if l == 0 else ADA_ROUTE)[-1])))
                gains(l, 0)
                rsqrt((l, "n1c"), D)
                normalise((l, "n1b"), l, 0)
                for i in range(2):
                    b = take(v, (l, f"cq{i}"))
                    evac((l, f"cq{i}"), tc(cq[:, i, :], b[:, 0:T]))
                b = take(v, (l, "ckv"))
                evac((l, "ckv"), tc(ckvT[:, 0:T], b[:, 0:T]))
                b = take(v, (l, "swk"))
                evac((l, "swk"), tc(swk[:, 0:T], b[:, 0:T]))
                read_out(v, (l, "swk"))
                is_filled(v, (l, "swq2"))
                tt(sqm[:, 0:2, :], cq, cq, ALU.mult)
                tt(sqm[:, 2, :], ckvT[:, 0:T], ckvT[:, 0:T], ALU.mult).then_inc(s_sqm, 1)
                rsqrt((l, "nqc"), QR)
                b = take(v, (l, "nqb"))
                for i in range(2):
                    ins = stt(cq[:, i, :], cq[:, i, :], vT[:, 1, 24 + 2 * l + i:25 + 2 * l + i], b[:, 0:T], ALU.mult, ALU.mult)
                evac((l, "nqb"), ins)
                rsqrt((l, "nkc"), KR)
                b = take(v, (l, "nkb"))
                evac((l, "nkb"), stt(ckvT[:, 0:T], ckvT[:, 0:T], vT[:, 1, 28 + l:29 + l], b[:, 0:T], ALU.mult, ALU.mult))

                def rope(j, x, swapped, angles, rows, tmp):
                    b = take(v, j)
                    cs, sn = (cv(a)[rows, :] for a in angles)
                    if len(x.shape) == 3:
                        cs = cs.unsqueeze(1).to_broadcast([cs.shape[0], x.shape[1], TS])
                        sn = sn.unsqueeze(1).to_broadcast([sn.shape[0], x.shape[1], TS])
                    evac(j, tt(tmp, swapped(b), sn, ALU.mult))
                    chain(tt(x, x, cs, ALU.mult))
                    return tt(x, x, tmp, ALU.add)

                full, mr = slice(0, P), slice(ND, QKD)
                sw, mla = ("cos", "sin"), ("cosm", "sinm")
                chain(rope((l, "rk"), swk[:, TP:T], lambda b: b[:, 0:TS], sw, full, ropet[:, 0, :]))
                rope((l, "rkp"), kpeT[mr, TP:T], lambda b: b[mr, 0:TS], mla, mr, ropet[mr, 1, :]).then_inc(s_kr, 1)
                for i in range(3):
                    chain(rope((l, f"rq{i}"), swq[:, i, TP:T], lambda b: b[:, 0:TS], sw, full, ropet[:, 0, :]))
                v.wait_ge(s_kr, l + 1)
                for i in range(3):
                    ins = rope((l, f"rm{i}"), mq[mr, 2 * i:2 * i + 2, TP:T], lambda b: b[mr, :].rearrange("p (a b) -> p a b", a=2),
                               mla, mr, ropet[mr, :, :])
                    if i < 2:
                        chain(ins)
                ins.then_inc(s_qkv, 1)
                if l == 0:
                    v.wait_ge(s_bs, 16 * 4)

                def top(u):
                    pair, s, g, h, t = UNITS[u]
                    r = u % 8
                    b = take(v, (l, f"S{u}"))
                    chain(nc.vector.tensor_reduce(st[:, r, 0:1], b[:, 0:P if t == 0 else T], AX.X, ALU.max))
                    ts(st[:, r, 1:2], st[:, r, 0:1], sinks[:, l, 2 * pair + s:2 * pair + s + 1], -1.0, ALU.max, ALU.mult)\
                        .then_inc(s_max, 1)

                def norm(u):
                    pair, s, g, h, t = UNITS[u]
                    n = P if t == 0 else T
                    r = u % 8
                    read_out(v, (l, f"S{u}"))
                    den = st[:, r, 2:3]
                    if g == "swa":
                        v.wait_ge(s_snk, l * 18 + u - 29)
                        chain(tt(st[:, r, 5:6], den, st[:, r, 3:4], ALU.add))
                        den = st[:, r, 5:6]
                    chain(nc.vector.reciprocal(st[:, r, 4:5], den))
                    ts(pr[:, u % 3, 0:n], pr[:, u % 3, 0:n], st[:, r, 4:5], None, ALU.mult).then_inc(s_nrm, 1)

                def out(pair):
                    v.wait_ge(s_pv, l * NU + 6 * (pair + 1))
                    tc(hT[:, pair, :], bO[pair % 2][:, 0:T]).then_inc(s_o, 1)

                for i in range(NU + LAG_PV + 1):
                    if i < NU:
                        top(i)
                    if 1 <= i <= NU:
                        norm(i - 1)
                    for j in ada_in_step(i) if l == 0 else []:
                        ada(l, j)
                    if i >= LAG_PV + 1 and (i - LAG_PV - 1) % 6 == 5:
                        out((i - LAG_PV - 1) // 6)

                for n in range(KT):
                    b = take(v, (l, f"op{n}"))
                    for cond in range(2):
                        x = zT[:, n, sel(cond)]
                        ins = stt(x, b[:, sel(cond)], modT[:, l, 16 + n, cond:cond + 1], x, ALU.mult, ALU.add)
                    evac((l, f"op{n}"), ins)
                read_out(v, (l, "op7"))
                read_out(v, (0, "B011"))
                gains(l, 1)
                rsqrt((l, "n2c"), D)
                for j in route[0:3]:
                    ada(l, j)
                normalise((l, "n2b"), l, 1)

                R = [rw[:, i, :] for i in range(12)]

                def g4(x):
                    return x.rearrange("p (g e) -> p g e", e=EPG)

                def te(x):
                    return x.rearrange("p (t e) -> p t e", t=NT)

                def spread4(x, which):
                    y = g4(x)
                    return (y.unsqueeze(2) if which == "i" else y.unsqueeze(3)).to_broadcast([P, y.shape[1], EPG, EPG])

                before = cv("before").rearrange("p (j i) -> p j i", j=EPG)

                def beaten(x, dst, n):
                    c1, c2 = cmp1[:, 0:n], cmp2[:, 0:n]
                    chain(tt(c1, spread4(x, "i"), spread4(x, "j"), ALU.is_equal))
                    chain(tt(c1, c1, before.unsqueeze(1).to_broadcast([P, n, EPG, EPG]), ALU.mult))
                    chain(tt(c2, spread4(x, "i"), spread4(x, "j"), ALU.is_gt))
                    chain(tt(c1, c1, c2, ALU.add))
                    chain(nc.vector.tensor_reduce(g4(dst), c1, AX.X, ALU.add))

                read_out(v, (l, "router"))
                chain(ts(R[1], R[0], 1.0, None, ALU.add))
                chain(nc.vector.reciprocal(R[2], R[1]))
                chain(tt(te(R[3]), te(R[2]), brt[:].unsqueeze(1).to_broadcast([P, NT, NE]), ALU.add))
                beaten(R[3], R[5], NT * NG)
                chain(ts(R[5], R[5], TOPK - 0.5, None, ALU.is_lt))
                chain(tt(R[6], R[3], R[5], ALU.mult))
                chain(nc.vector.tensor_reduce(R[7][:, 0:NT * NG], g4(R[6]), AX.X, ALU.add))
                beaten(R[7][:, 0:NT * NG], R[8][:, 0:NT * NG], NT)
                chain(ts(R[8][:, 0:NT * NG], R[8][:, 0:NT * NG], 0.5, None, ALU.is_lt))
                tt(g4(R[4]), g4(R[5]), R[8][:, 0:NT * NG].unsqueeze(2).to_broadcast([P, NT * NG, EPG]), ALU.mult)\
                    .then_inc(s_mask, 1)
                for j in route[3:6]:
                    ada(l, j)
                v.wait_ge(s_mask, l + 1)
                chain(tt(R[6], R[2], R[4], ALU.mult))
                chain(nc.vector.tensor_reduce(R[9][:, 0:NT], te(R[6]), AX.X, ALU.add))
                chain(nc.vector.reciprocal(R[9][:, 4:4 + NT], R[9][:, 0:NT]))
                tt(vals[:, :, :, 2], te(R[6]), R[9][:, 4:4 + NT].unsqueeze(2).to_broadcast([P, NT, NE]), ALU.mult)
                chain(tt(cmp1, spread4(R[4], "i"), before.unsqueeze(1).to_broadcast([P, NT * NG, EPG, EPG]), ALU.mult))
                chain(nc.vector.tensor_reduce(g4(R[10]), cmp1, AX.X, ALU.add))
                chain(ts(R[10], R[10], float(T), None, ALU.mult))
                tid = cv("tokid").unsqueeze(2).to_broadcast([P, NT, NE])
                tc(vals[:, :, :, 0], tid)
                chain(tt(vals[:, :, :, 1], te(R[10]), tid, ALU.add))
                b = take(v, (l, "rank"))
                chain(nc.vector.tensor_reduce(cnt[:, 0:1], b[:, 3 * NE:4 * NE], AX.X, ALU.max))
                tc(cnti[:, 0:1], cnt[:, 0:1]).then_inc(s_cnt, 1)
                evac((l, "rank"), ts(R[11], b[:, 0:NT * NE], 1.0, None, ALU.add))
                for j in route[6:]:
                    ada(l, j)
                read_out(v, (l, "rank"))
                chain(tt(R[11], R[11], R[4], ALU.mult))
                chain(ts(R[11], R[11], -1.0, None, ALU.add))

                def experts(p):
                    n = PASSES * l + p
                    if p:
                        ts(R[11], R[11], -float(P), None, ALU.add).then_inc(s_rest, 1)
                        v.wait_ge(s_rest, (PASSES - 1) * l + p)
                    rk = te(R[11])
                    for q in range(NG):
                        if q >= 2:
                            v.wait_ge(s_onehu, n * (NG - 1) + q - 1)
                        for t in range(NT):
                            ins = tt(onehot[:, q % 2, t], cv("iota").unsqueeze(1).to_broadcast([P, EPG, P]),
                                     rk[:, t, q * EPG:(q + 1) * EPG].unsqueeze(2).to_broadcast([P, EPG, P]), ALU.is_equal)
                        ins.then_inc(s_oneh, 1)
                    v.wait_ge(s_slotp, n + 1)
                    if p:
                        for k in range(2):
                            v.wait_ge(gathers(l, p - 1)[0][k], gathers(l, p - 1)[1][k] + G_PASS[k])
                            v.wait_ge(scatters(l, p - 1)[0][k], scatters(l, p - 1)[1] + SC_PASS)
                    sl = bA[:, 0:3 * NE].rearrange("p (e c) -> p e c", c=3)
                    ts(idxg[:, 0:NE], sl[:, :, 0], BIG, None, ALU.add)
                    ts(idxs[:, 0:NE], sl[:, :, 1], BIG, None, ALU.add)
                    tc(gsl[:], sl[:, :, 2]).then_inc(s_slot, 1)
                    v.wait_ge(s_slot, n + 1)

                    def activate(e, par):
                        tc(gcol[:, par:par + 1], gsl[:, e:e + 1] if isinstance(e, int) else gsl[:, bass.ds(e, 1)]).then_inc(s_gcol, 1)
                        v.wait_ge(s_gcol, n * NE + e + 1)
                        v.wait_ge(s_sg, n * NE + e + 1)
                        wait(v, s_at, n * NE + e)
                        stt(am, bU[:], gcol[:, par:par + 1], sg, ALU.mult, ALU.mult).then_inc(s_a, 1)

                    def turned(e):
                        v.wait_ge(s_at, n * NE + e + 1)
                        wait(v, s_y, n * NE + e)
                        tc(aTs, bA[:].rearrange("p (k s) -> p k s", k=4)).then_inc(s_as, 1)

                    def rows_out(e, par, stored):
                        v.wait_ge(s_y, n * NE + e + 1)
                        wait(v, scatters(l, p)[0][par], stored)
                        tc(ysb[:, par, 512:1024], bY[1][:]).then_inc(s_ysv, 1)

                    activate(0, 0)
                    turned(0)

                    def step(i, u):
                        e = 2 * i + 1 + u
                        activate(e, 1 - u)
                        rows_out(e - 1, u, scatters(l, p)[1] + 16 * i)
                        turned(e)
                    step(0, 0)
                    step(0, 1)
                    with v.Fori(1, NE // 2 - 1) as i:
                        step(i, 0)
                        step(i, 1)
                    step(NE // 2 - 1, 0)
                    rows_out(NE - 1, 1, scatters(l, p)[1] + SC_PASS - 16)

                experts(0)
                v.wait_ge(s_cnt, l + 1)
                most = v.value_load(cnti[0:1, 0:1], min_val=0, max_val=T)
                for p in range(1, PASSES):
                    with v.If(most > P * p):
                        experts(p)
                    with v.Else():
                        v.wait_ge(s_ysv, NE * (PASSES * l + p))
                        for s, k in ((s_rest, 1), (s_oneh, NG), (s_slot, 1), (s_gcol, NE), (s_a, NE), (s_as, NE), (s_ysv, NE)):
                            v.sem_inc(s, k)

                for t in range(NT):
                    v.wait_ge(s_yl[t], 16 * TOPK * (l + 1))
                    tt(yl[:, t, 0, :], yl[:, t, 0, :], yl[:, t, 1, :], ALU.add).then_inc(s_ysum, 1)
                for t in range(NT):
                    cond = 1 if t == 0 else 0
                    for h in range(2):
                        b = take(v, (l, f"y{t}{h}"))
                        for k in range(4):
                            x = zT[:, 4 * h + k, t * P:(t + 1) * P]
                            ins = stt(x, b[:, k * P:(k + 1) * P], modT[:, l, 40 + 4 * h + k, cond:cond + 1], x, ALU.mult, ALU.add)
                        evac((l, f"y{t}{h}"), ins)
                read_out(v, (l, "y21"))

            rsqrt("nfc", D)
            normalise("nfb", None, 0)
            for t in range(NT):
                b = take(v, f"fo{t}1")
                evac(f"fo{t}1", tc(xrows[:, t, 512:1024], b[:]))

        @block.gpsimd
        def _(g):
            g.dma_start(swaf, C_dram[:, KEPT_W:CONST_W]).then_inc(s_swaf, 16)
            bound_h, bound_y = g.to_reg(T - 1), g.to_reg(TOPK * T - 1)
            chain = Chain(g, s_chainp)
            nc.gpsimd.memset(sinks[:], -1e38)
            nc.gpsimd.memset(idxg[:, NE:NE + 1], int(BIG))
            chain(nc.gpsimd.memset(bpad[:], 0.0))
            for l in range(DEPTH):
                g.dma_start(sinks[:, l, 10:16], A["swa_sink"][l:l + 1, :].to_broadcast([P, SH])).then_inc(s_bs, 16)
            g.dma_start(brt[:], A["b_router"].rearrange("(o e) -> o e", o=1).to_broadcast([P, NE])).then_inc(s_bs, 16)
            g.dma_start(wr[:], A["w_router"].rearrange("(k p) e -> p k e", p=P)).then_inc(s_bs, 16)
            for i in range(DEPTH * NAH):
                g.dma_start(bpad[DRS * i:DRS * (i + 1), GW - NWW:GW + NWW - 1],
                            A["na_rpb"][i // NAH, i % NAH, NWH - GR:NWH + GR - 1, :]).then_inc(s_bp, 16)
            g.wait_ge(s_bp, 16 * DEPTH * NAH)
            nrow = DEPTH * NAH * DRS
            g.dma_start(bscr.rearrange("r (q c) -> r q c", q=GW), bpad[0:nrow, :].unsqueeze(1).to_broadcast([nrow, GW, TW]))\
                .then_inc(s_bscr, 16)

            for l in range(DEPTH):
                is_filled(g, "x21" if l == 0 else (l - 1, "y21"))
                if l == 0:
                    read_out(g, "vecB")
                chain(nc.gpsimd.memset(ckp[:, 0:ND], 0.0))
                for dst, src in ((cnk, A["cache_na_k"][0, l].rearrange("t h d -> t (h d)")), (cck, A["cache_mla_ckv"][0, l]),
                                 (csk, A["cache_swa_k"][0, l].rearrange("t h d -> t (h d)")), (ckp[:, ND:QKD], A["cache_mla_kpe"][0, l]),
                                 (vna[:, 3, :], A["cache_na_v"][0, l].rearrange("t h d -> t (h d)")),
                                 (swv[:, 3, :], A["cache_swa_v"][0, l].rearrange("t h d -> t (h d)"))):
                    g.dma_start(dst, src).then_inc(s_cache, 16)
                g.dma_start(wqb[:], A["w_mla_qb"][l].rearrange("(k p) n -> p k n", p=P)).then_inc(s_lat, 16)
                g.dma_start(wkvb[:], A["w_mla_kvb"][l]).then_inc(s_lat, 16)
                g.wait_ge(s_kr, l + 1)
                read_out(g, (l, "cache2"))
                nc.gpsimd.tensor_copy(mk[ND:QKD, :, :], kpeT[ND:QKD, :].unsqueeze(1).to_broadcast([RD, MH, TK])).then_inc(s_kpr, 1)
                read_out(g, (l, "rows2"))
                for name, src in (("new_na_k", rows_o[:, 0:2 * P]), ("new_mla_ckv", rows_o[:, 2 * P:3 * P]),
                                  ("new_swa_k", rows_o[:, 3 * P:4 * P]), ("new_mla_kpe", rows_o[:, 4 * P:4 * P + RD]),
                                  ("new_na_v", vna[:, 0, :]), ("new_swa_v", swv[:, 0, :])):
                    dst = O[name][0, l]
                    if len(dst.shape) == 3:
                        dst = dst.rearrange("t h d -> t (h d)")
                    g.dma_start(dst, src).then_inc(s_store, 16)
                g.wait_ge(s_store, 16 * 6 * (l + 1))
                if l == 0:
                    g.wait_ge(s_bscr, 16)
                for qr in range(GR):
                    for h in range(NAH):
                        src = bass.AP(bscr.tensor, ((l * NAH + h) * DRS + GR - 1 - qr) * GW * TW + GW - 1,
                                      [[TW - 1, GW], [GW * TW, GR], [1, GW]])
                        dst = bm[GW * (qr % 2):GW * (qr % 2 + 1), NAH * (qr // 2) + h, :]
                        g.dma_start(dst.rearrange("p (r c) -> p r c", r=GR), src).then_inc(s_bmd, 16)
                g.wait_ge(s_bmd, 16 * GR * NAH * (l + 1))
                b3 = bm.rearrange("p h (r c) -> p (h r) c", c=GW)
                g.wait_ge(s_kpr, l + 1)
                nc.gpsimd.tensor_tensor(b3, b3, cv("colmask").unsqueeze(1).to_broadcast([P, 2 * NAH * GR, GW]), ALU.add)\
                    .then_inc(s_bm, 1)

                g.wait_ge(s_hscr, 16 * NT * (l + 1))

                def experts(p):
                    n = PASSES * l + p
                    g.wait_ge(s_slot, n + 1)

                    for e in range(-2, NE):
                        if e + 2 <= NE:
                            wait(g, s_xt, n * (NE + 1) + max(e + 1, 0))
                            g.indirect_dma_start(grow[:, e % 2, :], None, hscr,
                                                 bass.IndirectOffsetOnAxis(ap=idxg[:, e + 2:e + 3], axis=0),
                                                 bounds_check=bound_h, oob_is_err=False).then_inc(gathers(l, p)[0][e % 2], 16)
                        if e < 0:
                            continue
                        g.wait_ge(s_ysv, n * NE + e + 1)
                        g.wait_ge(s_ysa, n * NE + e + 1)
                        g.indirect_dma_start(yscr, bass.IndirectOffsetOnAxis(ap=idxs[:, e:e + 1], axis=0), ysb[:, e % 2, :], None,
                                             bounds_check=bound_y, oob_is_err=False).then_inc(scatters(l, p)[0][e % 2], 16)

                experts(0)
                g.wait_ge(s_cnt, l + 1)
                most = g.value_load(cnti[0:1, 0:1], min_val=0, max_val=T)
                for p in range(1, PASSES):
                    with g.If(most > P * p):
                        experts(p)
                        for k in range(2):
                            g.wait_ge(gathers(l, p)[0][k], G_PASS[k])
                            g.wait_ge(scatters(l, p)[0][k], SC_PASS)
                        g.sem_inc(s_further, 1)
                    with g.Else():
                        g.sem_inc(s_further, 1)


INS = ["x_prompt", "x_sample", "c", "cache_na_k", "cache_na_v", "cache_mla_ckv", "cache_mla_kpe", "cache_swa_k",
       "cache_swa_v", "c_ctx", "w_ada", "b_ada", "g_attn", "w_in", "g_mla_q", "w_mla_qb", "g_mla_kv", "w_mla_kvb", "na_rpb",
       "swa_sink", "w_out", "g_ffn", "w_router", "b_router", "w_gate", "w_up", "w_down", "g_final"]
OUTS = [("y_prompt", (1, TP, D)), ("y_sample", (1, TS, D)), ("new_na_k", (1, DEPTH, TP, NAH, HD)),
        ("new_na_v", (1, DEPTH, TP, NAH, HD)), ("new_mla_ckv", (1, DEPTH, TP, KR)), ("new_mla_kpe", (1, DEPTH, TP, RD)),
        ("new_swa_k", (1, DEPTH, TP, SKV, HD)), ("new_swa_v", (1, DEPTH, TP, SKV, HD))]


def kernel(**inputs):
    import numpy as _np
    import concourse.bacc as _bacc
    from concourse import mybir as _mybir
    from concourse.bass_utils import run_bass_kernel_spmd as _run

    nc = _bacc.Bacc("TRN2", target_bir_lowering=False, num_devices=1)
    arrays, args = {}, {}
    for name in INS:
        a = _np.ascontiguousarray(inputs[name])
        arrays[f"in_{name}"] = a
        args[name] = nc.dram_tensor(f"in_{name}", a.shape, _mybir.dt.from_np(a.dtype), kind="ExternalInput").ap()
    arrays["constants"] = constants()
    consts = nc.dram_tensor("constants", arrays["constants"].shape, F32, kind="ExternalInput").ap()
    outs = {name: nc.dram_tensor(f"out_{name}", shape, F32, kind="ExternalOutput").ap() for name, shape in OUTS}
    build(nc, args, consts, outs)
    r = _run(nc, [arrays], core_ids=[0])
    return tuple(r.results[0][f"out_{name}"] for name, _ in OUTS)
```

```python
from contextlib import ExitStack

import numpy as np

import concourse.bass as bass
from concourse import mybir

F32 = mybir.dt.float32
F32R = mybir.dt.float32r
BF16 = mybir.dt.bfloat16
I32 = mybir.dt.int32
ALU = mybir.AluOpType
ACT = mybir.ActivationFunctionType
AX = mybir.AxisListType

P = 128
D = 1024
KT = D // P
DEPTH = 2
TP = 128
TS = 256
T = TP + TS
NT = T // P
TK = T + 128
GW = 64
GR = TS // GW
HD = 64
NAH, NWH, NWW = 4, 8, 16
MH, QR, KR, ND, RD, VD = 6, 256, 128, 64, 32, 64
QKD = ND + RD
SH, SKV = 6, 2
SWIN = 128
NE, NG, EPG, TOPK = 16, 4, 4, 2
DE = 512
EPS = 1e-6
NMOD = 6
NA_IN = 3 * NAH * HD
IN_W = NA_IN + QR + KR + RD + (SH + 2 * SKV) * HD
SCALE = HD ** -0.5
MSCALE = QKD ** -0.5
NEG = -1e30
BIG = 2048.0
TW = 2 * GW - 1
DRS = 2 * GR - 1

SLOTS = 6
CW = 4096
N_ADA, N_IN, N_OUT = 12, 4, 2
PASSES = NT
MOE_CH = 3 * NE

ADA_FIRST = [(0, c) for c in range(4)]
ADA_ATT = [(0, c) for c in range(4, N_ADA)] + [(1, c) for c in range(8)]
ADA_ROUTE = [(1, c) for c in range(8, N_ADA)]
ADA_ALL = ADA_FIRST + ADA_ATT + ADA_ROUTE
ATT_STEP = 3

STREAM = [[("in", i) for i in range(N_IN)] + [("out", i) for i in range(N_OUT)] for _ in range(DEPTH)]
STREAM[0] = ([("ada", *x) for x in ADA_FIRST] + STREAM[0][:N_IN] + [("ada", *x) for x in ADA_ATT] + STREAM[0][N_IN:]
             + [("ada", *x) for x in ADA_ROUTE])
MOE_AT = [len(x) for x in STREAM]
LAYER_AT = [0, MOE_AT[0] + MOE_CH]
assert all((a + b) % SLOTS == 0 for a, b in zip(MOE_AT, LAYER_AT)) and LAYER_AT[1] % SLOTS == 0
IN_PARTS = {2: 2, 3: 6}
NB = 6

CONST = {}
_at = 0
for _n, _w in (("ident", P), ("ones", P), ("tri", P), ("rot", P), ("rotm", QKD), ("iota", P), ("cos", TS), ("sin", TS),
               ("cosm", TS), ("sinm", TS), ("colmask", GW), ("before", 16), ("tokid", NT), ("swamask", 2 * TS)):
    CONST[_n] = (_at, _w)
    _at += _w
CONST_W = _at
KEPT_W = CONST_W - 2 * TS


def constants():
    c = np.zeros((P, CONST_W), np.float32)

    def put(name, v, rows=slice(0, P)):
        a, w = CONST[name]
        c[rows, a:a + w] = v

    i = np.arange(P)
    put("ident", np.eye(P))
    put("ones", 1.0)
    put("tri", (i[:, None] < i[None, :]))
    sw = (i // HD) * HD + (i % HD + HD // 2) % HD
    r = np.zeros((P, P))
    r[sw, i] = 1
    put("rot", r)
    r = np.zeros((QKD, QKD))
    j = np.arange(RD)
    r[ND + (j + RD // 2) % RD, ND + j] = 1
    put("rotm", r, slice(0, QKD))
    put("iota", i[None, :])
    t = np.arange(TS)
    row, col = (t // GW).astype(np.float32), (t % GW).astype(np.float32)

    def angles(rot):
        per = rot // 2
        inv = (np.float32(10000.0) ** (-np.arange(0, per, 2, dtype=np.float32) / np.float32(per))).astype(np.float32)
        return np.concatenate([row[:, None] * inv, col[:, None] * inv], axis=-1).astype(np.float32)

    a = angles(HD)
    cs, sn = np.cos(a).T, np.sin(a).T
    put("cos", np.concatenate([cs, cs, cs, cs]))
    put("sin", np.concatenate([-sn, sn, -sn, sn]))
    a = angles(RD)
    cs, sn = np.cos(a).T, np.sin(a).T
    put("cosm", np.concatenate([cs, cs]), slice(ND, QKD))
    put("sinm", np.concatenate([-sn, sn]), slice(ND, QKD))
    q = np.arange(GW)
    start = np.clip(q - NWW // 2, 0, GW - NWW)
    ok = (q[None, :] >= start[:, None]) & (q[None, :] < start[:, None] + NWW)
    put("colmask", np.where(np.concatenate([ok, ok]), 0.0, NEG))
    qp = np.arange(P)
    kp = np.arange(TS)
    put("swamask", np.concatenate([np.where(np.abs(kp[None, :] - (qt * P + qp[:, None])) <= SWIN, 0.0, NEG)
                                   for qt in range(2)], axis=1))
    e = np.arange(EPG)
    put("before", np.tile((e[None, :] < e[:, None]).astype(np.float32).reshape(1, 16), (P, 1)))
    put("tokid", i[:, None] + P * np.arange(NT)[None, :] - BIG)
    return c


def ada_jobs(chunks):
    rows, turned = [f"A{x}{c}" for x, c in chunks], [f"B{x}{c}" for x, c in chunks]
    return [rows[0]] + [j for pair in zip(rows[1:] + [None], turned) for j in pair if j]


def ada_in_step(i):
    k, r = divmod(i, ATT_STEP)
    if k >= len(ADA_ATT) or r not in (0, ATT_STEP // 2):
        return []
    x, c = ADA_ATT[k]
    return [f"{'B' if r else 'A'}{x}{c}"]


def job_order():
    order = ["vecA", "vecB"] + [f"x{t}{h}" for t in range(NT) for h in range(2)]
    for l in range(DEPTH):
        n = ["n1c"] + (ada_jobs(ADA_FIRST) if l == 0 else []) + ["n1b"]
        n += ["naq0", "naq1", "nak0", "nak1"] + [f"nav{t}" for t in range(NT)] + ["cq0", "cq1"]
        n += ["ckv", "kpe", "swk"] + [f"swv{t}" for t in range(NT)] + ["swq0", "swq1", "swq2"]
        n += ["cache1", "cache2", "nqc", "nkc", "nqb", "nkb", "rk", "rkp"]
        n += ["rq0", "rq1", "rq2"] + ["rows1", "rows2"]
        n += [f"mq{h}" for h in range(MH)] + [f"mk{h}" for h in range(MH)] + ["rm0", "rm1", "rm2"]
        n += [f"mv{t}" for t in range(4)]
        for i in range(len(UNITS) + LAG_PV):
            if i < len(UNITS):
                n.append(f"S{i}")
            if 0 <= i - LAG_T < len(UNITS):
                n.append(f"T{i - LAG_T}")
            if l == 0:
                n += ada_in_step(i)
        n += [f"op{k}" for k in range(KT)]
        r = ada_jobs(ADA_ROUTE) if l == 0 else []
        n += r[0:1] + ["n2c"] + r[1:3] + ["n2b", "router", "hr00", "routerT"] + [f"hr{t}{h}" for t in range(NT) for h in range(2)][1:]
        n += r[3:5] + ["rank"] + r[5:] + [f"y{t}{h}" for t in range(NT) for h in range(2)]
        order += [(l, j) for j in n]
    order += ["nfc", "nfb"] + [f"fo{t}{h}" for t in range(NT) for h in range(2)]
    return {j: k for k, j in enumerate(order)}


UNITS = []
for _pair in range(8):
    for _t in range(NT):
        for _s in range(2):
            _g, _h = (("na", 2 * _pair + _s) if _pair < 2 else ("mla", 2 * (_pair - 2) + _s) if _pair < 5
                      else ("swa", 2 * (_pair - 5) + _s))
            UNITS.append((_pair, _s, _g, _h, _t))
NU = len(UNITS)
LAG_T = 3
LAG_PV = 4
JOB = job_order()


def build(nc, A, C_dram, O):
    with ExitStack() as ctx:
        def sb(name, shape, dt=F32):
            return ctx.enter_context(nc.sbuf_tensor(name, shape, dt))

        def both(name, shape):
            with ExitStack() as first:
                plain = first.enter_context(nc.sbuf_tensor(name, shape, F32))
            return plain, sb(name + "_r", shape, F32R)

        def sem(name):
            return ctx.enter_context(nc.semaphore(name))

        ring, ring_r = zip(*(both(f"ring{i}", [P, CW]) for i in range(SLOTS)))
        cst = sb("cst", [P, KEPT_W])
        zT = sb("zT", [P, KT, T])
        hT = sb("hT", [P, KT, T])
        vT = sb("vT", [P, 2, P])
        modT = sb("modT", [P, DEPTH, 48, 2])
        gain = sb("gain", [P, 2, KT, 2])
        sil = sb("sil", [P, 3, 16])
        sil32 = sb("sil32", [P, KT, 32])
        arow = sb("arow", [P, 512])
        identb = sb("identb", [P, P], BF16)
        swab = sb("swab", [P, 2 * TS], BF16)
        sinks = sb("sinks", [P, DEPTH, 16])
        ns = sb("ns", [P, 6, NT])
        diag = sb("diag", [P, NT, P])
        st = sb("st", [P, 8, 6])
        wr = sb("wr", [P, KT, NE])
        brt = sb("brt", [P, NE])
        cnt = sb("cnt", [P, 4])
        cnti = sb("cnti", [P, 2], I32)
        idxg = sb("idxg", [P, NE + 1], I32)
        idxs = sb("idxs", [P, NE + 1], I32)
        gsl = sb("gsl", [P, NE])
        gcol = sb("gcol", [P, 2])
        wqb = sb("wqb", [P, 2, MH * QKD])
        wkvb = sb("wkvb", [P, MH * (ND + VD)])
        WORK = 16384
        work, work_r = both("work", [P, WORK])

        at = [0]

        def carve(n, base=None, src=work):
            if base is not None:
                at[0] = base
            a = at[0]
            at[0] += n
            assert at[0] <= WORK, at[0]
            return src[:, a:a + n]

        def c3(v, a):
            return v.rearrange("p (a b) -> p a b", a=a)

        xrows = c3(carve(NT * D, 0), NT)
        vecs = c3(carve(2 * P), 2)
        swaf = carve(2 * TS)
        qna = c3(carve(2 * T, 0), 2)
        kna = c3(carve(2 * TK), 2)
        vna = c3(carve(4 * NAH * HD), 4)
        kpeT = carve(TK)
        mq = c3(carve(MH * T), MH)
        mk = c3(carve(MH * TK), MH)
        mv = c3(carve(4 * MH * VD), 4)
        swq = c3(carve(3 * T), 3)
        swk = carve(TK)
        swv = c3(carve(4 * SKV * HD), 4)
        bm_at = at[0]
        bm = c3(carve(2 * NAH * TS), 2 * NAH)
        pr_at = at[0]
        pr3 = c3(carve(3 * T), 3)
        pr = [pr3[:, 0], pr3[:, 1], pr3[:, 2], kpeT[:, 0:T]]
        pt = c3(carve(2 * T), 2)
        cnk = carve(NAH * HD, bm_at)
        cck = carve(KR)
        csk = carve(SKV * HD)
        ckp = carve(QKD)
        cq = c3(carve(2 * T, pr_at), 2)
        ropet = c3(carve(2 * TS), 2)
        ckvT = carve(TK)
        bpad = carve(TW)
        sqm = hT
        rows_o = hT[:, 6:8, :].rearrange("p a b -> p (a b)")[:, 0:4 * P + RD]
        grow = c3(carve(2 * D, 0), 2)
        xs_hi, xs_lo = (c3(carve(D, src=work_r), KT) for _ in range(2))
        ysb = c3(carve(2 * D), 2)
        sa = carve(DE)
        aT_hi, aT_lo = (c3(carve(DE, src=work_r), 4) for _ in range(2))
        yl_at = at[0]
        w_hi = c3(carve(2 * CW, src=work_r), 2)
        vals = carve(NT * NE * 4, src=work_r).rearrange("p (t e c) -> p t e c", t=NT, e=NE)
        rank = carve(NT * NE)
        wr32 = c3(carve(KT * 32), KT)
        onehot = carve(2 * NT * EPG * P, 2 * D, work_r).rearrange("p (b t e s) -> p b t e s", b=2, t=NT, e=EPG)
        rw = c3(carve(12 * 48), 12)
        cmp1 = carve(192).rearrange("p (g j i) -> p g j i", j=4, i=4)
        cmp2 = carve(192).rearrange("p (g j i) -> p g j i", j=4, i=4)
        assert at[0] <= 6 * D
        hrow = [grow[:, 0, :], grow[:, 1, :], carve(D, 6 * D)]
        rlog = carve(T)
        yl = carve(2 * NT * D, yl_at).rearrange("p (t k d) -> p t k d", t=NT, k=2)

        def cv(name):
            a, w = CONST[name]
            return cst[:, a:a + w]

        ident, ones = cv("ident"), cv("ones")

        hscr = nc.dram_tensor("hscr", [T, D], F32, kind="Internal").ap()
        yscr = nc.dram_tensor("yscr", [TOPK * T, D], F32, kind="Internal").ap()
        bscr = nc.dram_tensor("bscr", [DEPTH * NAH * DRS, GW * TW], F32, kind="Internal").ap()

        banks = [ctx.enter_context(nc.psum_tensor(f"bank{b}", [P, 512], F32)) for b in range(8)]
        bO = banks[6:8]
        bX, bG, bU, bA, bY = banks[0:2], banks[2], banks[3], banks[4], banks[5:7]

        s_const = sem("s_const")
        s_vec = sem("s_vec")
        s_swaf = sem("s_swaf")
        s_x = [sem(f"s_x{i}") for i in range(3)]
        s_chainv = sem("s_chainv")
        s_chaina = sem("s_chaina")
        s_chainp = sem("s_chainp")
        s_silx = sem("s_silx")
        s_sil = sem("s_sil")
        s_mod = sem("s_mod")
        s_sq = sem("s_sq")
        s_part = sem("s_part")
        s_diag = sem("s_diag")
        s_xn = sem("s_xn")
        s_hv = sem("s_hv")
        s_ha = sem("s_ha")
        s_cache = sem("s_cache")
        s_lat = sem("s_lat")
        s_bs = sem("s_bs")
        s_bp = sem("s_bp")
        s_bscr = sem("s_bscr")
        s_bmd = sem("s_bmd")
        s_bm = sem("s_bm")
        s_sqm = sem("s_sqm")
        s_kr = sem("s_kr")
        s_qkv = sem("s_qkv")
        s_kpr = sem("s_kpr")
        s_store = sem("s_store")
        s_max = sem("s_max")
        s_snk = sem("s_snk")
        s_nrm = sem("s_nrm")
        s_pv = sem("s_pv")
        s_o = sem("s_o")
        s_hscr = sem("s_hscr")
        s_wr = sem("s_wr")
        s_rexp = sem("s_rexp")
        s_mask = sem("s_mask")
        s_cnt = sem("s_cnt")
        s_oneh = sem("s_oneh")
        s_onehu = sem("s_onehu")
        s_slotp = sem("s_slotp")
        s_slot = sem("s_slot")
        s_gcol = sem("s_gcol")
        s_rest = sem("s_rest")
        s_g = [sem(f"s_g{i}") for i in range(2)]
        s_xt = sem("s_xt")
        s_xh = sem("s_xh")
        s_xs = sem("s_xs")
        s_hi = sem("s_hi")
        s_lo = sem("s_lo")
        s_hu = sem("s_hu")
        s_gd = sem("s_gd")
        s_gu = sem("s_gu")
        s_sg = sem("s_sg")
        s_a = sem("s_a")
        s_at = sem("s_at")
        s_ah = sem("s_ah")
        s_as = sem("s_as")
        s_y = sem("s_y")
        s_ys = sem("s_ys")
        s_sc = [sem(f"s_sc{i}") for i in range(2)]
        s_yl = [sem(f"s_yl{i}") for i in range(3)]
        s_ysum = sem("s_ysum")
        s_out = sem("s_out")
        s_gf = {(l, p): [sem(f"s_g_{l}{p}{i}") for i in range(2)] for l in range(DEPTH) for p in range(1, PASSES)}
        s_scf = {(l, p): [sem(f"s_sc_{l}{p}{i}") for i in range(2)] for l in range(DEPTH) for p in range(1, PASSES)}
        s_further = sem("s_further")
        s_land = [sem(f"s_land{i}") for i in range(SLOTS)]
        s_land2 = [sem(f"s_landf{i}") for i in range(SLOTS)]
        s_fill = [sem(f"s_fill{b}") for b in range(NB)]
        s_evac = [sem(f"s_evac{b}") for b in range(NB)]

        def wait(eng, s, v):
            if isinstance(v, int) and v <= 0:
                return
            eng.wait_ge(s, v)

        def bank(j):
            return banks[JOB[j] % NB]

        def fill_begin(j):
            wait(nc.tensor, s_evac[JOB[j] % NB], JOB[j] // NB)
            return bank(j)

        def filled(j, ins):
            ins.then_inc(s_fill[JOB[j] % NB], 1)

        def take(eng, j):
            eng.wait_ge(s_fill[JOB[j] % NB], JOB[j] // NB + 1)
            return bank(j)

        def evac(j, ins):
            ins.then_inc(s_evac[JOB[j] % NB], 1)

        def is_filled(eng, j):
            eng.wait_ge(s_fill[JOB[j] % NB], JOB[j] // NB + 1)

        def read_out(eng, j):
            eng.wait_ge(s_evac[JOB[j] % NB], JOB[j] // NB + 1)

        class Chain:

            def __init__(self, eng, s):
                self.eng, self.s, self.n = eng, s, 0

            def __call__(self, ins):
                self.n += 1
                ins.then_inc(self.s, 1)
                self.eng.wait_ge(self.s, self.n)

        def landed(l, k):
            slot, n = k % SLOTS, LAYER_AT[l] + k
            more = sum(parts - 1 for l2 in range(l + 1) for i, parts in IN_PARTS.items()
                       for at_ in [STREAM[l2].index(("in", i))] if at_ % SLOTS == slot and LAYER_AT[l2] + at_ <= n)
            return slot, 16 * (n // SLOTS + 1 + more)

        def arrived(eng, l, name):
            slot, v = landed(l, STREAM[l].index(name))
            eng.wait_ge(s_land[slot], v)
            return ring[slot][:]

        def sel(cond):
            return slice(TP, T) if cond == 0 else slice(0, TP)

        block = ctx.enter_context(nc.Block())

        def place(e_half, kind):
            pos = 3 * (1 + e_half) - 1 + kind
            return pos % SLOTS, pos // SLOTS

        def moe_land(l, p, slot, use):
            if p == 0:
                return s_land[slot], landed(l, MOE_AT[l] + SLOTS * use + slot)[1]
            return s_land2[slot], 16 * ((MOE_CH // SLOTS) * ((PASSES - 1) * l + p - 1) + use + 1)

        G_PASS = (16 * (NE // 2 + 1), 16 * (NE // 2))
        SC_PASS = 16 * (NE // 2)

        def chunk_no(l, p, e, kind):
            first = MOE_CH * (PASSES * l + p)
            if isinstance(e, int) and e in (0, NE):
                return first + (kind if e == 0 else MOE_CH - 1)
            return 3 * e - 1 + kind + first

        def gathers(l, p):
            return (s_g, [l * k for k in G_PASS]) if p == 0 else (s_gf[l, p], [0, 0])

        def scatters(l, p):
            return (s_sc, l * SC_PASS) if p == 0 else (s_scf[l, p], 0)

        def last_reader(l, k):
            kind, *x = STREAM[l][k]
            if kind == "ada":
                return (l, f"A{x[0]}{x[1]}")
            return (l, {"in": ("nak1", "cq1", "swv2", "swq2"), "out": ("op3", "op7")}[kind][x[0]])

        def ring_after_experts(sp, slot, n):
            s, back = ((s_gu, 1), (s_y, 2), (s_gd, 0), (s_gu, 0), (s_y, 1), (s_y, 0))[slot]
            sp.wait_ge(s, n * NE - back)

        wg_d = A["w_gate"].rearrange("l e (p k) n -> l e p (k n)", p=P)
        wu_d = A["w_up"].rearrange("l e (p k) n -> l e p (k n)", p=P)
        wd_d = A["w_down"].rearrange("l e (p k) n -> l e p (k n)", p=P)

        @block.sync
        def _(sp):
            sp.dma_start(cst[:], C_dram[:, 0:KEPT_W]).then_inc(s_const, 16)
            row = 0
            for name, n in (("b_ada", DEPTH * 48), ("g_attn", DEPTH * KT), ("g_ffn", DEPTH * KT)):
                sp.dma_start(vecs[row:row + n, 0, :], A[name].rearrange("l (j p) -> (l j) p", p=P)).then_inc(s_vec, 16)
                row += n
            sp.dma_start(vecs[0:8, 1, :], A["c"].rearrange("o (j p) -> (o j) p", p=P)).then_inc(s_vec, 16)
            sp.dma_start(vecs[8:16, 1, :], A["c_ctx"].rearrange("(j p) -> j p", p=P)).then_inc(s_vec, 16)
            sp.dma_start(vecs[16:24, 1, :], A["g_final"].rearrange("(j p) -> j p", p=P)).then_inc(s_vec, 16)
            sp.dma_start(vecs[24:28, 1, :], A["g_mla_q"].rearrange("l (j p) -> (l j) p", p=P)).then_inc(s_vec, 16)
            sp.dma_start(vecs[28:30, 1, :], A["g_mla_kv"]).then_inc(s_vec, 16)
            for t in range(NT):
                src = A["x_prompt"][0] if t == 0 else A["x_sample"][0, (t - 1) * P:t * P, :]
                sp.dma_start(xrows[:, t, :], src).then_inc(s_x[t], 16)

            def chunk(l, k, parts):
                slot = k % SLOTS
                if k >= SLOTS:
                    is_filled(sp, last_reader(l, k - SLOTS))
                elif l > 0:
                    if k == 2:
                        sp.wait_ge(s_yl[NT - 1], 16 * TOPK * l)
                    ring_after_experts(sp, slot, PASSES * (l - 1) + 1)
                for dst, src in parts(ring[slot][:]):
                    sp.dma_start(dst, src).then_inc(s_land[slot], 16)

            def cols(w, c, n):
                def parts(r):
                    return [(r[:, 0:KT * n].rearrange("p (k n) -> p k n", k=KT),
                             w.rearrange("(k p) n -> p k n", p=P)[:, :, c:c + n])]
                return parts

            def in_tail(l):
                w = A["w_in"][l].rearrange("(k p) n -> p k n", p=P)
                a = NA_IN + QR
                b = a + KR + RD + SH * HD

                def parts(r):
                    v = r[:, 0:KT * 416].rearrange("p (k n) -> p k n", k=KT)
                    return [(v[:, :, 0:KR + RD], w[:, :, a:a + KR + RD]), (v[:, :, KR + RD:416], w[:, :, b:b + 256])]
                return parts

            def in_swq(l):
                w = A["w_in"][l].rearrange("(k p) n -> p k n", p=P)
                a = NA_IN + QR + KR + RD

                def parts(r):
                    v = r[:, 0:KT * 384].rearrange("p (k h s d) -> p k h s d", k=KT, h=3, s=2)
                    return [(v[:, :, h, s, :], w[:, :, a + (3 * s + h) * HD:a + (3 * s + h + 1) * HD])
                            for h in range(3) for s in range(2)]
                return parts

            for l in range(DEPTH):
                w_in = (cols(A["w_in"][l], 0, 512), cols(A["w_in"][l], 512, 512), in_tail(l), in_swq(l))
                for k, (kind, *x) in enumerate(STREAM[l]):
                    if kind == "ada":
                        chunk(l, k, cols(A["w_ada"][x[0]], x[1] * 512, 512))
                    elif kind == "in":
                        chunk(l, k, w_in[x[0]])
                    else:
                        chunk(l, k, cols(A["w_out"][l], x[0] * 512, 512))

                def load(l, p, slot, use, w, e):
                    src = w[l, e] if isinstance(e, int) else w[l, bass.ds(e, 1)].rearrange("a p n -> (a p) n")
                    sp.dma_start(ring[slot][:], src).then_inc(moe_land(l, p, slot, 0)[0], 16)

                def stream(p):
                    n = PASSES * l + p

                    def before(slot):
                        if p == 0:
                            is_filled(sp, last_reader(l, MOE_AT[l] - SLOTS + slot))
                        else:
                            ring_after_experts(sp, slot, n)
                    before(0)
                    load(l, p, 0, 0, wg_d, 0)
                    before(1)
                    load(l, p, 1, 0, wu_d, 0)

                    def step(i, u):
                        e = 2 * i + 1 + u
                        for kind, (w, s, back) in enumerate(((wg_d, s_gd, 1), (wu_d, s_gu, 1), (wd_d, s_y, 2))):
                            slot, use = place(u, kind)
                            if isinstance(i, int) and i == 0 and use == 0:
                                before(slot)
                            elif isinstance(i, int) and i == 0:
                                sp.wait_ge((s_gd, s_gu)[slot], n * NE + 1)
                            else:
                                sp.wait_ge(s, e + n * NE - back)
                            load(l, p, slot, use, w, e - (kind == 2))
                    step(0, 0)
                    step(0, 1)
                    with sp.Fori(1, NE // 2 - 1) as i:
                        step(i, 0)
                        step(i, 1)
                    step(NE // 2 - 1, 0)
                    sp.wait_ge(s_gd, n * NE + NE - 1)
                    load(l, p, 5, 0, wd_d, NE - 1)
                    if p:
                        sp.wait_ge(s_y, (n + 1) * NE)

                stream(0)
                sp.wait_ge(s_cnt, l + 1)
                most = sp.value_load(cnti[0:1, 0:1], min_val=0, max_val=T)
                for p in range(1, PASSES):
                    with sp.If(most > P * p):
                        stream(p)
                    with sp.Else():
                        for slot, s in enumerate(s_land2):
                            before_n = (PASSES - 1) * l + p - 1
                            wait(sp, s, 16 * (MOE_CH // SLOTS) * before_n)
                            sp.sem_inc(s, 16 * MOE_CH // SLOTS)

            for t in range(NT):
                read_out(sp, f"fo{t}0")
                read_out(sp, f"fo{t}1")
                dst = O["y_prompt"][0] if t == 0 else O["y_sample"][0, (t - 1) * P:t * P, :]
                sp.dma_start(dst, xrows[:, t, :]).then_inc(s_out, 16)
            sp.wait_ge(s_out, 16 * NT)
            sp.wait_ge(s_store, 16 * 6 * DEPTH)

        @block.tensor
        def _(pe):
            mm = nc.tensor.matmul
            turn_ = nc.tensor.transpose

            def turn4(j, src):
                b = fill_begin(j)
                for k in range(4):
                    last = turn_(b[:, k * P:(k + 1) * P], src(k), ident)
                filled(j, last)

            def partition_sums(j, n):
                pe.wait_ge(s_part, n)
                b = fill_begin(j)
                for t in range(NT):
                    last = mm(b[:, t:t + 1], diag[:, t, :], ones[:, 0:1], start=True, stop=True)
                filled(j, last)

            def sums(j, sq, nk):
                b = fill_begin(j)
                for t in range(NT):
                    for k in range(nk):
                        last = mm(b[:, t:t + 1], sq[:, k, t * P:(t + 1) * P], ones[:, 0:1], start=(k == 0), stop=(k == nk - 1))
                filled(j, last)

            def spread(j, n):
                pe.wait_ge(s_diag, n)
                b = fill_begin(j)
                filled(j, mm(b[:, 0:T], ones, diag[:].rearrange("p t q -> p (t q)"), start=True, stop=True))

            pe.wait_ge(s_const, 16)
            pe.wait_ge(s_vec, 16 * 8)
            b = fill_begin("vecA")
            filled("vecA", turn_(b[:, 0:P], vecs[:, 0, :], ident))
            b = fill_begin("vecB")
            filled("vecB", turn_(b[:, 0:30], vecs[0:30, 1, :], ident[0:30, 0:30]))
            for t in range(NT):
                pe.wait_ge(s_x[t], 16)
                for h in range(2):
                    turn4(f"x{t}{h}", lambda k: xrows[:, t, (4 * h + k) * P:(4 * h + k + 1) * P])
            pe.wait_ge(s_sil, 1)

            for l in range(DEPTH):
                def ada(j):
                    kind, x, c = j[0], int(j[1]), int(j[2:])
                    if kind == "A":
                        w = arrived(pe, l, ("ada", x, c)).rearrange("p (k n) -> p k n", k=KT)
                        b = fill_begin((l, j))
                        for k in range(KT):
                            last = mm(b[32 * (k % 4):32 * (k % 4) + 32, :], sil32[:, k, :], w[:, k, :], start=(k < 4), stop=(k >= 4),
                                      skip_group_check=True)
                    else:
                        read_out(pe, (l, f"A{x}{c}"))
                        b = fill_begin((l, j))
                        for k in range(4):
                            last = turn_(b[:, k * P:(k + 1) * P], arow[:, k * P:(k + 1) * P], ident)
                    filled((l, j), last)

                route = ada_jobs(ADA_ROUTE) if l == 0 else []

                def proj(name, w, c, m):
                    b = fill_begin((l, name))
                    for k in range(KT):
                        last = mm(b[0:m, 0:T], w[:, k, c:c + m], hT[:, k, :], start=(k == 0), stop=(k == KT - 1))
                    filled((l, name), last)

                def proj_rows(name, w, c, m, t):
                    b = fill_begin((l, name))
                    for k in range(KT):
                        last = mm(b[:, 0:m], hT[:, k, t * P:(t + 1) * P], w[:, k, c:c + m], start=(k == 0), stop=(k == KT - 1))
                    filled((l, name), last)

                partition_sums((l, "n1c"), 2 * l + 1)
                for j in ada_jobs(ADA_FIRST) if l == 0 else []:
                    ada(j)
                spread((l, "n1b"), 4 * l + 1)
                pe.wait_ge(s_hv, 2 * l + 1)
                pe.wait_ge(s_ha, 2 * l + 1)
                w = arrived(pe, l, ("in", 0)).rearrange("p (k n) -> p k n", k=KT)
                for i, name in enumerate(("naq0", "naq1", "nak0", "nak1")):
                    proj(name, w, i * P, P)
                w = arrived(pe, l, ("in", 1)).rearrange("p (k n) -> p k n", k=KT)
                for t in range(NT):
                    proj_rows(f"nav{t}", w, 0, NAH * HD, t)
                for i in range(2):
                    proj(f"cq{i}", w, NAH * HD + i * P, P)
                w = arrived(pe, l, ("in", 2))[:, 0:KT * 416].rearrange("p (k n) -> p k n", k=KT)
                proj("ckv", w, 0, KR)
                proj("kpe", w, KR - ND, QKD)
                proj("swk", w, KR + RD, P)
                for t in range(NT):
                    proj_rows(f"swv{t}", w, KR + RD + P, P, t)
                w = arrived(pe, l, ("in", 3))[:, 0:KT * 384].rearrange("p (k n) -> p k n", k=KT)
                for i in range(3):
                    proj(f"swq{i}", w, i * P, P)
                pe.wait_ge(s_cache, 16 * 6 * (l + 1))
                turn4((l, "cache1"), lambda k: (cnk[:, 0:P], cnk[:, P:2 * P], cck, csk)[k])
                b = fill_begin((l, "cache2"))
                filled((l, "cache2"), turn_(b[0:QKD, 0:P], ckp, ident))
                pe.wait_ge(s_sqm, l + 1)
                sums((l, "nqc"), sqm[:, 0:2, :], 2)
                sums((l, "nkc"), sqm[:, 2:3, :], 1)
                spread((l, "nqb"), 4 * l + 2)
                spread((l, "nkb"), 4 * l + 3)
                read_out(pe, (l, "swk"))
                b = fill_begin((l, "rk"))
                filled((l, "rk"), mm(b[:, 0:TS], cv("rot"), swk[:, TP:T], start=True, stop=True))
                read_out(pe, (l, "kpe"))
                b = fill_begin((l, "rkp"))
                filled((l, "rkp"), mm(b[0:QKD, 0:TS], cv("rotm")[0:QKD, :], kpeT[0:QKD, TP:T], start=True, stop=True))
                read_out(pe, (l, "swq2"))
                for i in range(3):
                    b = fill_begin((l, f"rq{i}"))
                    filled((l, f"rq{i}"), mm(b[:, 0:TS], cv("rot"), swq[:, i, TP:T], start=True, stop=True))
                read_out(pe, (l, "nkb"))
                turn4((l, "rows1"), lambda k: (kna[:, 0, 0:P], kna[:, 1, 0:P], ckvT[:, 0:P], swk[:, 0:P])[k])
                b = fill_begin((l, "rows2"))
                filled((l, "rows2"), turn_(b[:, 0:QKD], kpeT[0:QKD, 0:P], ident[0:QKD, 0:QKD]))
                pe.wait_ge(s_lat, 16 * 2 * (l + 1))
                read_out(pe, (l, "cache1"))
                for h in range(MH):
                    b = fill_begin((l, f"mq{h}"))
                    for k in range(2):
                        last = mm(b[0:QKD, 0:T], wqb[:, k, h * QKD:(h + 1) * QKD], cq[:, k, :], start=(k == 0), stop=(k == 1))
                    filled((l, f"mq{h}"), last)
                for h in range(MH):
                    b = fill_begin((l, f"mk{h}"))
                    filled((l, f"mk{h}"), mm(b[0:ND, :], wkvb[:, h * P:h * P + ND], ckvT, start=True, stop=True))
                for i in range(3):
                    read_out(pe, (l, f"mq{2 * i + 1}"))
                    b = fill_begin((l, f"rm{i}"))
                    filled((l, f"rm{i}"), mm(b[0:QKD, :], cv("rotm")[0:QKD, :],
                                             mq[0:QKD, 2 * i:2 * i + 2, TP:T], start=True, stop=True))
                vcols = wkvb[:].rearrange("p (h c) -> p h c", h=MH)[:, :, ND:]
                for t in range(4):
                    b = fill_begin((l, f"mv{t}"))
                    filled((l, f"mv{t}"), mm(b[:, 0:MH * VD], ckvT[:, t * P:(t + 1) * P], vcols, start=True, stop=True))

                pe.wait_ge(s_qkv, l + 1)
                read_out(pe, (l, "mv3"))
                pe.wait_ge(s_kpr, l + 1)
                pe.wait_ge(s_bm, l + 1)

                def scores(u):
                    pair, s, g, h, t = UNITS[u]
                    q = slice(t * P, (t + 1) * P)
                    ks = slice(0, TP) if t == 0 else slice(TP, TK)
                    n = ks.stop - ks.start
                    b = fill_begin((l, f"S{u}"))
                    if g == "na":
                        r = slice(64 * (h % 2), 64 * (h % 2) + 64)
                        lhs, rhs = qna[r, h // 2, q], kna[r, h // 2, ks]
                    elif g == "mla":
                        lhs, rhs = mq[0:QKD, h, q], mk[0:QKD, h, ks]
                    else:
                        r = slice(64 * (h // 3), 64 * (h // 3) + 64)
                        lhs, rhs = swq[r, h % 3, q], swk[r, ks]
                    masked = t > 0 and g != "mla"
                    last = mm(b[:, 0:n], lhs, rhs, start=True, stop=True)
                    if masked and g == "na":
                        last = mm(b[:, 0:TS], ident, bm[:, (t - 1) * NAH + h, :], start=False, stop=True, skip_group_check=True)
                    elif masked:
                        last = mm(b[:, 0:TS], identb[:], swab[:, (t - 1) * TS:t * TS], start=False, stop=True, skip_group_check=True)
                    filled((l, f"S{u}"), last)

                def turn(u):
                    pe.wait_ge(s_nrm, l * NU + u + 1)
                    b = fill_begin((l, f"T{u}"))
                    for c in range(1 if UNITS[u][4] == 0 else 3):
                        last = turn_(b[:, c * P:(c + 1) * P], pr[u % 4][:, c * P:(c + 1) * P], ident)
                    filled((l, f"T{u}"), last)

                def values(u):
                    pair, s, g, h, t = UNITS[u]
                    read_out(pe, (l, f"T{u}"))
                    if t == 0 and s == 0:
                        wait(pe, s_o, l * 8 + pair - 1)
                    o = bO[pair % 2][64 * s:64 * s + 64, t * P:(t + 1) * P]
                    chunks = (0,) if t == 0 else (1, 2, 3)
                    for i, c in enumerate(chunks):
                        v = (vna[:, c, h * HD:(h + 1) * HD] if g == "na" else mv[:, c, h * VD:(h + 1) * VD] if g == "mla"
                             else swv[:, c, (h // 3) * HD:(h // 3 + 1) * HD])
                        last = mm(o, v, pt[:, u % 2, i * P:(i + 1) * P], start=(i == 0), stop=(i == len(chunks) - 1))
                    last.then_inc(s_pv, 1)

                for i in range(NU + LAG_PV):
                    if i < NU:
                        scores(i)
                    if 0 <= i - LAG_T < NU:
                        turn(i - LAG_T)
                    for j in ada_in_step(i) if l == 0 else []:
                        ada(j)
                    if i >= LAG_PV:
                        values(i - LAG_PV)

                pe.wait_ge(s_o, 8 * (l + 1))
                for n in range(KT):
                    if n % 4 == 0:
                        w = arrived(pe, l, ("out", n // 4)).rearrange("p (k n) -> p k n", k=KT)
                    proj(f"op{n}", w, (n % 4) * P, P)
                for j in route[0:1]:
                    ada(j)
                partition_sums((l, "n2c"), 2 * l + 2)
                for j in route[1:3]:
                    ada(j)
                spread((l, "n2b"), 4 * l + 4)
                pe.wait_ge(s_hv, 2 * l + 2)
                pe.wait_ge(s_ha, 2 * l + 2)
                if l == 0:
                    pe.wait_ge(s_bs, 16 * 4)
                pe.wait_ge(s_wr, 2 * (l + 1))
                b = fill_begin((l, "router"))
                for k in range(KT):
                    last = mm(b[32 * (k % 4):32 * (k % 4) + 32, 0:T], wr32[:, k, :], hT[:, k, :], start=(k < 4), stop=(k >= 4),
                              skip_group_check=True)
                filled((l, "router"), last)
                turn4((l, "hr00"), lambda k: hT[:, k, 0:P])
                read_out(pe, (l, "router"))
                b = fill_begin((l, "routerT"))
                for t in range(NT):
                    last = turn_(b[:, t * P:(t + 1) * P], rlog[:, t * P:(t + 1) * P], ident)
                filled((l, "routerT"), last)
                for i in range(1, 2 * NT):
                    t, h = divmod(i, 2)
                    turn4((l, f"hr{t}{h}"), lambda k: hT[:, 4 * h + k, t * P:(t + 1) * P])
                for j in route[3:5]:
                    ada(j)
                pe.wait_ge(s_mask, l + 1)
                m = rw[:, 4, :].rearrange("p (t e) -> p t e", t=NT)
                b = fill_begin((l, "rank"))
                for t in range(NT):
                    for t2 in range(t):
                        mm(b[:, t * NE:(t + 1) * NE], ones, m[:, t2, :], start=(t2 == 0), stop=False)
                    mm(b[:, t * NE:(t + 1) * NE], cv("tri"), m[:, t, :], start=(t == 0), stop=True)
                for t in range(NT):
                    last = mm(b[:, 3 * NE:4 * NE], ones, m[:, t, :], start=(t == 0), stop=(t == NT - 1))
                filled((l, "rank"), last)
                for j in route[5:]:
                    ada(j)
                for bk in range(NB):
                    done = max(n for n in range(JOB[(l, "y00")]) if n % NB == bk)
                    pe.wait_ge(s_evac[bk], done // NB + 1)

                def experts(p):
                    n = PASSES * l + p
                    for q in range(NG):
                        pe.wait_ge(s_oneh, n * NG + q + 1)
                        for t in range(NT):
                            for e in range(EPG):
                                c = (q * EPG + e) * 4
                                last = mm(bA[:, c:c + 4], onehot[:, q % 2, t, e, :], vals[:, t, q * EPG + e, :],
                                          start=(q == 0 and t == 0 and e == 0), stop=(t == NT - 1), skip_group_check=True)
                        last.then_inc(s_onehu if q < NG - 1 else s_slotp, 1)

                    def tokens(e, par, land):
                        pe.wait_ge(gathers(l, p)[0][par], land)
                        wait(pe, s_xs, n * (NE + 1) + e)
                        for k in range(KT):
                            last = turn_(bX[k // 4][:, (k % 4) * P:(k % 4 + 1) * P], grow[:, par, k::KT], ident)
                        last.then_inc(s_xt, 1)

                    def product(outs, x_hi, x_lo, slot, m, done):
                        nk = CW // 512 // len(outs)
                        hi, lo = (w.rearrange("p (k b n) -> p k b n", k=nk, n=512) for w in (w_hi[:, slot % 2, :], ring_r[slot][:]))
                        pe.wait_ge(s_hi, m + 1)
                        for half, b in enumerate(outs):
                            for k in range(nk):
                                mm(b[:], x_hi[:, k, :], hi[:, k, half, :], start=(k == 0), stop=False)
                                last = mm(b[:], x_lo[:, k, :], hi[:, k, half, :], start=False, stop=False)
                        last.then_inc(s_hu, 1)
                        pe.wait_ge(s_lo, m + 1)
                        for half, b in enumerate(outs):
                            for k in range(nk):
                                last = mm(b[:], x_hi[:, k, :], lo[:, k, half, :], start=False, stop=(k == nk - 1))
                        last.then_inc(done, 1)

                    def gate_up(e, slots):
                        pe.wait_ge(s_xs, n * (NE + 1) + e + 1)
                        wait(pe, s_a, n * NE + e)
                        product([bG], xs_hi, xs_lo, slots[0], chunk_no(l, p, e, 0), s_gd)
                        product([bU], xs_hi, xs_lo, slots[1], chunk_no(l, p, e, 1), s_gu)

                    def down(e, slot):
                        pe.wait_ge(s_as, n * NE + e + 1)
                        wait(pe, s_ys, n * NE + e)
                        product(bY, aT_hi, aT_lo, slot, chunk_no(l, p, e + 1, 2), s_y)

                    def turn_a(e):
                        pe.wait_ge(s_a, n * NE + e + 1)
                        for k in range(4):
                            last = turn_(bA[:, k * P:(k + 1) * P], sa[:, k::4], ident)
                        last.then_inc(s_at, 1)

                    g0, g1 = gathers(l, p)[1]
                    tokens(0, 0, g0 + 16)
                    gate_up(0, (0, 1))
                    tokens(1, 1, g1 + 16)
                    pe.wait_ge(s_slot, n + 1)
                    turn_a(0)

                    def step(i, u):
                        e = 2 * i + 1 + u
                        gate_up(e, [place(u, kind)[0] for kind in range(2)])
                        tokens(e + 1, u, (g0 if u == 0 else g1) + 16 * i + 32)
                        down(e - 1, place(u, 2)[0])
                        turn_a(e)
                    step(0, 0)
                    step(0, 1)
                    with pe.Fori(1, NE // 2 - 1) as i:
                        step(i, 0)
                        step(i, 1)
                    step(NE // 2 - 1, 0)
                    down(NE - 1, SLOTS - 1)

                experts(0)
                pe.wait_ge(s_cnt, l + 1)
                most = pe.value_load(cnti[0:1, 0:1], min_val=0, max_val=T)
                for p in range(1, PASSES):
                    with pe.If(most > P * p):
                        experts(p)
                    with pe.Else():
                        pe.wait_ge(s_y, NE * (PASSES * l + p))
                        for s, k in ((s_onehu, NG - 1), (s_slotp, 1), (s_xt, NE + 1), (s_hu, MOE_CH), (s_gd, NE), (s_gu, NE), (s_at, NE),
                                     (s_y, NE)):
                            pe.sem_inc(s, k)
                done = PASSES * (l + 1)
                pe.wait_ge(s_xs, done * (NE + 1))
                pe.wait_ge(s_as, done * NE)
                pe.wait_ge(s_ys, done * NE)
                for t in range(NT):
                    pe.wait_ge(s_ysum, l * NT + t + 1)
                    for h in range(2):
                        turn4((l, f"y{t}{h}"), lambda k: yl[:, t, 0, (4 * h + k) * P:(4 * h + k + 1) * P])

            partition_sums("nfc", 2 * DEPTH + 1)
            spread("nfb", 4 * DEPTH + 1)
            pe.wait_ge(s_hv, 2 * DEPTH + 1)
            for t in range(NT):
                for h in range(2):
                    turn4(f"fo{t}{h}", lambda k: hT[:, 4 * h + k, t * P:(t + 1) * P])

        @block.scalar
        def _(act):
            A_ = nc.scalar.activation
            act.wait_ge(s_silx, 1)
            A_(sil[:, 1, :], sil[:, 0, :], ACT.Exp, scale=-1.0).then_inc(s_silx, 1)

            def copy(j, dst, n, rows=slice(0, P), scale=1.0):
                b = take(act, j)
                src = b[rows, 0:n]
                if len(dst.shape) == 3:
                    src = src.rearrange("p (a b) -> p a b", a=dst.shape[1])
                evac(j, A_(dst, src, ACT.Copy, scale=scale))

            for t in range(NT):
                copy(f"x{t}1", zT[:, 4:8, t * P:(t + 1) * P], 512)

            def squares():
                for k in range(0, KT, 4):
                    last = A_(hT[:, k:k + 4, :], zT[:, k:k + 4, :], ACT.Square)
                last.then_inc(s_sq, 1)

            def modulate(l, which):
                act.wait_ge(s_xn, 2 * l + which + 1)
                for k in range(4):
                    for cond in range(2):
                        x = hT[:, k, sel(cond)]
                        last = A_(x, x, ACT.Identity, bias=modT[:, l, 24 * which + k, cond:cond + 1],
                                  scale=gain[:, which, k, cond:cond + 1])
                last.then_inc(s_ha, 1)

            def ada_row(l, j):
                if j[0] == "A":
                    before = ADA_ALL.index((int(j[1]), int(j[2:]))) - 1
                    if before >= 0:
                        is_filled(act, (l, "B{}{}".format(*ADA_ALL[before])))
                    copy((l, j), arow[:], 512)

            for l in range(DEPTH):
                route = ada_jobs(ADA_ROUTE) if l == 0 else []
                if l == 0:
                    read_out(act, "x20")
                    read_out(act, "x21")
                else:
                    read_out(act, (l - 1, "y21"))
                squares()
                for j in ada_jobs(ADA_FIRST) if l == 0 else []:
                    ada_row(l, j)
                modulate(l, 0)
                for i in range(2):
                    copy((l, f"naq{i}"), qna[:, i, :], T, scale=SCALE)
                for i in range(2):
                    copy((l, f"nak{i}"), kna[:, i, 0:T], T)
                for t in range(NT):
                    copy((l, f"nav{t}"), vna[:, t, :], NAH * HD)
                copy((l, "kpe"), kpeT[0:QKD, 0:T], T, rows=slice(0, QKD))
                for t in range(NT):
                    copy((l, f"swv{t}"), swv[:, t, :], P)
                for i in range(3):
                    copy((l, f"swq{i}"), swq[:, i, :], T, scale=SCALE)
                b = take(act, (l, "cache1"))
                A_(kna[:, :, T:TK], b[:, 0:2 * P].rearrange("p (a b) -> p a b", a=2), ACT.Copy)
                A_(ckvT[:, T:TK], b[:, 2 * P:3 * P], ACT.Copy)
                evac((l, "cache1"), A_(swk[:, T:TK], b[:, 3 * P:4 * P], ACT.Copy))
                copy((l, "cache2"), kpeT[0:QKD, T:TK], P, rows=slice(0, QKD))
                if l == 0:
                    act.wait_ge(s_bscr, 16)
                for qr in range(GR):
                    for h in range(NAH):
                        src = bass.AP(bscr.tensor, ((l * NAH + h) * DRS + GR - 1 - qr) * GW * TW + GW - 1,
                                      [[TW - 1, GW], [GW * TW, GR], [1, GW]])
                        dst = bm[GW * (qr % 2):GW * (qr % 2 + 1), NAH * (qr // 2) + h, :]
                        act.dma_start(dst.rearrange("p (r c) -> p r c", r=GR), src).then_inc(s_bmd, 16)
                copy((l, "rows1"), rows_o[:, 0:4 * P], 4 * P)
                b = take(act, (l, "rows2"))
                evac((l, "rows2"), A_(rows_o[:, 4 * P:4 * P + RD], b[:, ND:QKD], ACT.Copy))
                for h in range(MH):
                    copy((l, f"mq{h}"), mq[0:QKD, h, :], T, rows=slice(0, QKD), scale=MSCALE)
                for h in range(MH):
                    copy((l, f"mk{h}"), mk[0:ND, h, :], TK, rows=slice(0, ND))
                for t in range(4):
                    copy((l, f"mv{t}"), mv[:, t, :], MH * VD)

                def exps(u):
                    pair, s, g, h, t = UNITS[u]
                    n = P if t == 0 else T
                    r = u % 8
                    if u >= 4:
                        is_filled(act, (l, f"T{u - 4}"))
                    if u == 0:
                        is_filled(act, (l, "mv3"))
                        act.wait_ge(s_qkv, l + 1)
                    if u == 3:
                        act.wait_ge(s_kpr, l + 1)
                        is_filled(act, (l, "rows2"))
                    act.wait_ge(s_max, l * NU + u + 1)
                    b = take(act, (l, f"S{u}"))
                    evac((l, f"S{u}"), A_(pr[u % 4][:, 0:n], b[:, 0:n], ACT.Exp, bias=st[:, r, 1:2], accum_out=st[:, r, 2:3]))
                    if g == "swa":
                        A_(st[:, r, 3:4], sinks[:, l, 2 * pair + s:2 * pair + s + 1], ACT.Exp, bias=st[:, r, 1:2]).then_inc(s_snk, 1)

                def turned(u):
                    n = P if UNITS[u][4] == 0 else T
                    if u >= 2:
                        act.wait_ge(s_pv, l * NU + u - 1)
                    copy((l, f"T{u}"), pt[:, u % 2, 0:n], n)

                for i in range(NU + LAG_T):
                    if i < NU:
                        exps(i)
                    if i >= LAG_T:
                        turned(i - LAG_T)
                    for j in ada_in_step(i) if l == 0 else []:
                        ada_row(l, j)

                read_out(act, (l, "op7"))
                squares()
                for j in route[0:3]:
                    ada_row(l, j)
                modulate(l, 1)
                copy((l, "router"), rlog, T)
                read_out(act, (l, "routerT"))
                A_(rw[:, 0, :], rw[:, 0, :], ACT.Exp, scale=-1.0).then_inc(s_rexp, 1)
                for t in range(NT):
                    copy((l, f"hr{t}0"), hrow[t][:, 0:512], 512)
                    copy((l, f"hr{t}1"), hrow[t][:, 512:1024], 512)
                    read_out(act, (l, f"hr{t}1"))
                    act.dma_start(hscr[t * P:(t + 1) * P, :], hrow[t]).then_inc(s_hscr, 16)
                for j in route[3:]:
                    ada_row(l, j)

                def experts(p):
                    n = PASSES * l + p

                    def upper(e, kind, slot, i=0, use=0):
                        m = chunk_no(l, p, e, kind)
                        s, v = moe_land(l, p, slot, use)
                        act.wait_ge(s, v + 16 * i)
                        if not (isinstance(e, int) and e == 0):
                            act.wait_ge(s_hu, m - 1)
                            act.wait_ge(s_lo, m - 1)
                        A_(w_hi[:, slot % 2, :], ring[slot][:], ACT.Copy).then_inc(s_hi, 1)

                    def tokens_upper(e):
                        act.wait_ge(s_xt, n * (NE + 1) + e + 1)
                        wait(act, s_gu, n * NE + e)
                        A_(xs_hi[:, 0:4, :], bX[0][:].rearrange("p (k s) -> p k s", k=4), ACT.Copy)
                        A_(xs_hi[:, 4:8, :], bX[1][:].rearrange("p (k s) -> p k s", k=4), ACT.Copy).then_inc(s_xh, 1)

                    def silu(e):
                        act.wait_ge(s_gd, n * NE + e + 1)
                        wait(act, s_at, n * NE + e)
                        A_(sa, bG[:], ACT.Silu).then_inc(s_sg, 1)

                    def turned_upper(e):
                        act.wait_ge(s_at, n * NE + e + 1)
                        wait(act, s_y, n * NE + e)
                        A_(aT_hi, bA[:].rearrange("p (k s) -> p k s", k=4), ACT.Copy).then_inc(s_ah, 1)

                    def rows_out(e, par, stored):
                        act.wait_ge(s_y, n * NE + e + 1)
                        wait(act, scatters(l, p)[0][par], stored)
                        A_(ysb[:, par, 0:512], bY[0][:], ACT.Copy)
                        A_(ysb[:, par, 512:1024], bY[1][:], ACT.Copy).then_inc(s_ys, 1)

                    wait(act, s_y, n * NE)
                    upper(0, 0, 0)
                    upper(0, 1, 1)
                    tokens_upper(0)
                    upper(1, 0, place(0, 0)[0], 0, place(0, 0)[1])
                    silu(0)
                    tokens_upper(1)
                    upper(1, 1, place(0, 1)[0], 0, place(0, 1)[1])
                    turned_upper(0)

                    def step(i, u, last=False):
                        e = 2 * i + 1 + u
                        slot, use = place(u, 2)
                        upper(e, 2, slot, i, use)
                        silu(e)
                        if not last:
                            slot, use = place(1 - u, 0)
                            upper(e + 1, 0, slot, i + u, use)
                        tokens_upper(e + 1)
                        if not last:
                            slot, use = place(1 - u, 1)
                            upper(e + 1, 1, slot, i + u, use)
                        rows_out(e - 1, u, scatters(l, p)[1] + 16 * i)
                        turned_upper(e)
                    step(0, 0)
                    step(0, 1)
                    with act.Fori(1, NE // 2 - 1) as i:
                        step(i, 0)
                        step(i, 1)
                    step(NE // 2 - 1, 0, last=True)
                    upper(NE, 2, SLOTS - 1, 0, NE // 2 - 1)
                    rows_out(NE - 1, 1, scatters(l, p)[1] + SC_PASS - 16)

                experts(0)
                act.wait_ge(s_cnt, l + 1)
                most = act.value_load(cnti[0:1, 0:1], min_val=0, max_val=T)
                for p in range(1, PASSES):
                    with act.If(most > P * p):
                        experts(p)
                    with act.Else():
                        act.wait_ge(s_ys, NE * (PASSES * l + p))
                        for s, k in ((s_xh, NE + 1), (s_hi, MOE_CH), (s_sg, NE), (s_ah, NE), (s_ys, NE)):
                            act.sem_inc(s, k)
                act.wait_ge(s_sc[0], (l + 1) * SC_PASS)
                act.wait_ge(s_sc[1], (l + 1) * SC_PASS)
                act.wait_ge(s_further, (PASSES - 1) * (l + 1))
                for t in range(NT):
                    for k in range(TOPK):
                        act.dma_start(yl[:, t, k, :], yscr[k * T + t * P:k * T + (t + 1) * P, :]).then_inc(s_yl[t], 16)

            read_out(act, (DEPTH - 1, "y21"))
            squares()
            for t in range(NT):
                copy(f"fo{t}0", xrows[:, t, 0:512], 512)

        @block.vector
        def _(v):
            tt, ts, stt, tc = (nc.vector.tensor_tensor, nc.vector.tensor_scalar, nc.vector.scalar_tensor_tensor,
                               nc.vector.tensor_copy)
            chain = Chain(v, s_chainv)
            v.wait_ge(s_const, 16)
            tc(identb[:], ident)
            v.wait_ge(s_swaf, 16)
            tc(swab[:], swaf)
            for name, i, n in (("vecA", 0, P), ("vecB", 1, 30)):
                b = take(v, name)
                evac(name, tc(vT[:, i, 0:n], b[:, 0:n]))
            read_out(v, "vecB")
            tc(sil[:, 0, :], vT[:, 1, 0:16]).then_inc(s_silx, 1)
            v.wait_ge(s_silx, 2)
            chain(ts(sil[:, 2, :], sil[:, 1, :], 1.0, None, ALU.add))
            chain(nc.vector.reciprocal(sil[:, 1, :], sil[:, 2, :]))
            nc.vector.memset(sil32[:, :, 2:32], 0.0)
            tt(sil32[:, :, 0:2].rearrange("p k c -> p c k"), sil[:, 0, :].rearrange("p (c k) -> p c k", c=2),
               sil[:, 1, :].rearrange("p (c k) -> p c k", c=2), ALU.mult).then_inc(s_sil, 1)
            for t in range(NT):
                b = take(v, f"x{t}0")
                evac(f"x{t}0", tc(zT[:, 0:4, t * P:(t + 1) * P], b[:].rearrange("p (a b) -> p a b", a=4)))
            read_out(v, "x20")
            read_out(v, "x21")

            def feature_sums(n):
                v.wait_ge(s_sq, n)
                nc.vector.tensor_reduce(diag[:].rearrange("p t q -> p (t q)"), hT[:].rearrange("p k t -> p t k"), AX.X, ALU.add)\
                    .then_inc(s_part, 1)

            def rsqrt(j, nfeat):
                b = take(v, j)
                x, y, t1, t2, xh = ns[:, 0, :], ns[:, 1, :], ns[:, 2, :], ns[:, 3, :], ns[:, 5, :]
                evac(j, ts(x, b[:, 0:NT], 1.0 / nfeat, EPS, ALU.mult, ALU.add))
                read_out(v, j)
                chain(ts(ns[:, 4, :].bitcast(I32), x.bitcast(I32), 1, None, ALU.logical_shift_right))
                ts(xh, x, -0.5, None, ALU.mult)
                chain(ts(y.bitcast(I32), ns[:, 4, :].bitcast(I32), -1.0, 1597463007.0, ALU.mult, ALU.add))
                for _ in range(3):
                    chain(tt(t1, y, y, ALU.mult))
                    chain(tt(t2, t1, xh, ALU.mult))
                    chain(stt(y, t2, 1.5, y, ALU.add, ALU.mult))
                for t in range(NT):
                    ins = ts(diag[:, t, :], ident, y[:, t:t + 1], None, ALU.mult)
                ins.then_inc(s_diag, 1)

            def ada(l, j):
                if j[0] == "B":
                    x, c = int(j[1]), int(j[2:])
                    b = take(v, (l, j))
                    mod = modT[:, x, 4 * c:4 * c + 4, :]
                    partial = b[:].rearrange("p (j g r) -> p j r g", j=4, g=4)[:, :, 0:2, :]
                    evac((l, j), nc.vector.tensor_reduce(mod, partial, AX.X, ALU.add))
                    read_out(v, (l, j))
                    tt(mod, mod, vT[:, 0, x * 48 + 4 * c:x * 48 + 4 * c + 4].unsqueeze(2).to_broadcast([P, 4, 2]), ALU.add)\
                        .then_inc(s_mod, 1)

            def gains(l, which):
                a = 96 + 16 * which + l * KT
                g = vT[:, 0, a:a + KT].unsqueeze(2).to_broadcast([P, KT, 2])
                chain(ts(gain[:, which], modT[:, l, 24 * which + 8:24 * which + 16, :], 1.0, None, ALU.add))
                chain(tt(gain[:, which], gain[:, which], g, ALU.mult))

            def normalise(j, l, which):
                b = take(v, j)
                half = b[:, 0:T].unsqueeze(1).to_broadcast([P, 4, T])
                ins = tt(hT[:, 0:4, :], zT[:, 0:4, :], half, ALU.mult)
                if l is not None:
                    ins.then_inc(s_xn, 1)
                evac(j, tt(hT[:, 4:8, :], zT[:, 4:8, :], half, ALU.mult))
                read_out(v, j)
                if l is None:
                    for k in range(KT):
                        ins = ts(hT[:, k, :], hT[:, k, :], vT[:, 1, 16 + k:17 + k], None, ALU.mult)
                else:
                    for k in range(4, KT):
                        for cond in range(2):
                            x = hT[:, k, sel(cond)]
                            ins = ts(x, x, gain[:, which, k, cond:cond + 1], modT[:, l, 24 * which + k, cond:cond + 1],
                                     ALU.mult, ALU.add)
                ins.then_inc(s_hv, 1)

            for l in range(DEPTH):
                route = ada_jobs(ADA_ROUTE) if l == 0 else []
                feature_sums(2 * l + 1)
                rsqrt((l, "n1c"), D)
                for j in ada_jobs(ADA_FIRST) if l == 0 else []:
                    ada(l, j)
                v.wait_ge(s_mod, len(ADA_FIRST if l == 0 else ADA_ALL))
                gains(l, 0)
                normalise((l, "n1b"), l, 0)
                for i in range(2):
                    b = take(v, (l, f"cq{i}"))
                    evac((l, f"cq{i}"), tc(cq[:, i, :], b[:, 0:T]))
                b = take(v, (l, "ckv"))
                evac((l, "ckv"), tc(ckvT[:, 0:T], b[:, 0:T]))
                b = take(v, (l, "swk"))
                evac((l, "swk"), tc(swk[:, 0:T], b[:, 0:T]))
                read_out(v, (l, "swk"))
                is_filled(v, (l, "swq2"))
                tt(sqm[:, 0:2, :], cq, cq, ALU.mult)
                tt(sqm[:, 2, :], ckvT[:, 0:T], ckvT[:, 0:T], ALU.mult).then_inc(s_sqm, 1)
                rsqrt((l, "nqc"), QR)
                b = take(v, (l, "nqb"))
                for i in range(2):
                    ins = stt(cq[:, i, :], cq[:, i, :], vT[:, 1, 24 + 2 * l + i:25 + 2 * l + i], b[:, 0:T], ALU.mult, ALU.mult)
                evac((l, "nqb"), ins)
                rsqrt((l, "nkc"), KR)
                b = take(v, (l, "nkb"))
                evac((l, "nkb"), stt(ckvT[:, 0:T], ckvT[:, 0:T], vT[:, 1, 28 + l:29 + l], b[:, 0:T], ALU.mult, ALU.mult))

                def rope(j, x, swapped, angles, rows, tmp):
                    b = take(v, j)
                    cs, sn = (cv(a)[rows, :] for a in angles)
                    if len(x.shape) == 3:
                        cs = cs.unsqueeze(1).to_broadcast([cs.shape[0], x.shape[1], TS])
                        sn = sn.unsqueeze(1).to_broadcast([sn.shape[0], x.shape[1], TS])
                    evac(j, tt(tmp, swapped(b), sn, ALU.mult))
                    chain(tt(x, x, cs, ALU.mult))
                    return tt(x, x, tmp, ALU.add)

                full, mr = slice(0, P), slice(ND, QKD)
                sw, mla = ("cos", "sin"), ("cosm", "sinm")
                chain(rope((l, "rk"), swk[:, TP:T], lambda b: b[:, 0:TS], sw, full, ropet[:, 0, :]))
                rope((l, "rkp"), kpeT[mr, TP:T], lambda b: b[mr, 0:TS], mla, mr, ropet[mr, 1, :]).then_inc(s_kr, 1)
                for i in range(3):
                    chain(rope((l, f"rq{i}"), swq[:, i, TP:T], lambda b: b[:, 0:TS], sw, full, ropet[:, 0, :]))
                v.wait_ge(s_kr, l + 1)
                for i in range(3):
                    ins = rope((l, f"rm{i}"), mq[mr, 2 * i:2 * i + 2, TP:T], lambda b: b[mr, :].rearrange("p (a b) -> p a b", a=2),
                               mla, mr, ropet[mr, :, :])
                    if i < 2:
                        chain(ins)
                ins.then_inc(s_qkv, 1)
                if l == 0:
                    v.wait_ge(s_bs, 16 * 4)

                def top(u):
                    pair, s, g, h, t = UNITS[u]
                    r = u % 8
                    b = take(v, (l, f"S{u}"))
                    chain(nc.vector.tensor_reduce(st[:, r, 0:1], b[:, 0:P if t == 0 else T], AX.X, ALU.max))
                    ts(st[:, r, 1:2], st[:, r, 0:1], sinks[:, l, 2 * pair + s:2 * pair + s + 1], -1.0, ALU.max, ALU.mult)\
                        .then_inc(s_max, 1)

                def norm(u):
                    pair, s, g, h, t = UNITS[u]
                    n = P if t == 0 else T
                    r = u % 8
                    read_out(v, (l, f"S{u}"))
                    den = st[:, r, 2:3]
                    if g == "swa":
                        v.wait_ge(s_snk, l * 18 + u - 29)
                        chain(tt(st[:, r, 5:6], den, st[:, r, 3:4], ALU.add))
                        den = st[:, r, 5:6]
                    chain(nc.vector.reciprocal(st[:, r, 4:5], den))
                    ts(pr[u % 4][:, 0:n], pr[u % 4][:, 0:n], st[:, r, 4:5], None, ALU.mult).then_inc(s_nrm, 1)

                def out(pair):
                    if pair == 6:
                        v.wait_ge(s_store, 16 * 6 * (l + 1))
                    v.wait_ge(s_pv, l * NU + 6 * (pair + 1))
                    tc(hT[:, pair, :], bO[pair % 2][:, 0:T]).then_inc(s_o, 1)

                for i in range(NU + LAG_PV + 1):
                    if i < NU:
                        top(i)
                    if 1 <= i <= NU:
                        norm(i - 1)
                    for j in ada_in_step(i) if l == 0 else []:
                        ada(l, j)
                    if i >= LAG_PV + 1 and (i - LAG_PV - 1) % 6 == 5:
                        out((i - LAG_PV - 1) // 6)

                for n in range(KT):
                    b = take(v, (l, f"op{n}"))
                    for cond in range(2):
                        x = zT[:, n, sel(cond)]
                        ins = stt(x, b[:, sel(cond)], modT[:, l, 16 + n, cond:cond + 1], x, ALU.mult, ALU.add)
                    evac((l, f"op{n}"), ins)
                read_out(v, (l, "op7"))
                v.wait_ge(s_mod, len(ADA_FIRST) + N_ADA - 4)
                gains(l, 1)
                feature_sums(2 * l + 2)
                rsqrt((l, "n2c"), D)
                for j in route[0:3]:
                    ada(l, j)
                normalise((l, "n2b"), l, 1)

                R = [rw[:, i, :] for i in range(12)]

                def g4(x):
                    return x.rearrange("p (g e) -> p g e", e=EPG)

                def te(x):
                    return x.rearrange("p (t e) -> p t e", t=NT)

                def spread4(x, which):
                    y = g4(x)
                    return (y.unsqueeze(2) if which == "i" else y.unsqueeze(3)).to_broadcast([P, y.shape[1], EPG, EPG])

                before = cv("before").rearrange("p (j i) -> p j i", j=EPG)

                def beaten(x, dst, n):
                    c1, c2 = cmp1[:, 0:n], cmp2[:, 0:n]
                    chain(tt(c1, spread4(x, "i"), spread4(x, "j"), ALU.is_equal))
                    chain(tt(c1, c1, before.unsqueeze(1).to_broadcast([P, n, EPG, EPG]), ALU.mult))
                    chain(tt(c2, spread4(x, "i"), spread4(x, "j"), ALU.is_gt))
                    chain(tt(c1, c1, c2, ALU.add))
                    chain(nc.vector.tensor_reduce(g4(dst), c1, AX.X, ALU.add))

                b = take(v, (l, "routerT"))
                evac((l, "routerT"), nc.vector.tensor_reduce(
                    te(R[0]), b[:, 0:T].rearrange("p (t g r) -> p t r g", t=NT, g=4)[:, :, 0:NE, :], AX.X, ALU.add))
                v.wait_ge(s_rexp, l + 1)
                chain(ts(R[1], R[0], 1.0, None, ALU.add))
                chain(nc.vector.reciprocal(R[2], R[1]))
                chain(tt(te(R[3]), te(R[2]), brt[:].unsqueeze(1).to_broadcast([P, NT, NE]), ALU.add))
                beaten(R[3], R[5], NT * NG)
                chain(ts(R[5], R[5], TOPK - 0.5, None, ALU.is_lt))
                chain(tt(R[6], R[3], R[5], ALU.mult))
                chain(nc.vector.tensor_reduce(R[7][:, 0:NT * NG], g4(R[6]), AX.X, ALU.add))
                beaten(R[7][:, 0:NT * NG], R[8][:, 0:NT * NG], NT)
                chain(ts(R[8][:, 0:NT * NG], R[8][:, 0:NT * NG], 0.5, None, ALU.is_lt))
                tt(g4(R[4]), g4(R[5]), R[8][:, 0:NT * NG].unsqueeze(2).to_broadcast([P, NT * NG, EPG]), ALU.mult)\
                    .then_inc(s_mask, 1)
                for j in route[3:5]:
                    ada(l, j)
                v.wait_ge(s_mask, l + 1)
                chain(tt(R[6], R[2], R[4], ALU.mult))
                chain(nc.vector.tensor_reduce(R[9][:, 0:NT], te(R[6]), AX.X, ALU.add))
                chain(nc.vector.reciprocal(R[9][:, 4:4 + NT], R[9][:, 0:NT]))
                chain(tt(te(R[6]), te(R[6]), R[9][:, 4:4 + NT].unsqueeze(2).to_broadcast([P, NT, NE]), ALU.mult))
                chain(tc(vals[:, :, :, 2], te(R[6])))
                tt(vals[:, :, :, 3], te(R[6]), vals[:, :, :, 2].bitcast(F32), ALU.subtract)
                chain(tt(cmp1, spread4(R[4], "i"), before.unsqueeze(1).to_broadcast([P, NT * NG, EPG, EPG]), ALU.mult))
                chain(nc.vector.tensor_reduce(g4(R[10]), cmp1, AX.X, ALU.add))
                chain(ts(R[10], R[10], float(T), None, ALU.mult))
                tid = cv("tokid").unsqueeze(2).to_broadcast([P, NT, NE])
                tc(vals[:, :, :, 0], tid)
                chain(tt(vals[:, :, :, 1], te(R[10]), tid, ALU.add))
                b = take(v, (l, "rank"))
                chain(nc.vector.tensor_reduce(cnt[:, 0:1], b[:, 3 * NE:4 * NE], AX.X, ALU.max))
                tc(cnti[:, 0:1], cnt[:, 0:1]).then_inc(s_cnt, 1)
                evac((l, "rank"), ts(rank, b[:, 0:NT * NE], 1.0, None, ALU.add))
                for j in route[5:]:
                    ada(l, j)
                read_out(v, (l, "rank"))
                chain(tt(rank, rank, R[4], ALU.mult))
                chain(ts(rank, rank, -1.0, None, ALU.add))

                def experts(p):
                    n = PASSES * l + p
                    if p:
                        ts(rank, rank, -float(P), None, ALU.add).then_inc(s_rest, 1)
                        v.wait_ge(s_rest, (PASSES - 1) * l + p)
                        v.wait_ge(s_y, n * NE)
                        for k in range(2):
                            v.wait_ge(gathers(l, p - 1)[0][k], gathers(l, p - 1)[1][k] + G_PASS[k])
                            v.wait_ge(scatters(l, p - 1)[0][k], scatters(l, p - 1)[1] + SC_PASS)
                    rk = te(rank)
                    for q in range(NG):
                        if q >= 2:
                            v.wait_ge(s_onehu, n * (NG - 1) + q - 1)
                        for t in range(NT):
                            ins = tt(onehot[:, q % 2, t], cv("iota").unsqueeze(1).to_broadcast([P, EPG, P]),
                                     rk[:, t, q * EPG:(q + 1) * EPG].unsqueeze(2).to_broadcast([P, EPG, P]), ALU.is_equal)
                        ins.then_inc(s_oneh, 1)
                    v.wait_ge(s_slotp, n + 1)
                    sl = bA[:, 0:4 * NE].rearrange("p (e c) -> p e c", c=4)
                    ts(idxg[:, 0:NE], sl[:, :, 0], BIG, None, ALU.add)
                    ts(idxs[:, 0:NE], sl[:, :, 1], BIG, None, ALU.add)
                    nc.vector.tensor_reduce(gsl[:], sl[:, :, 2:4], AX.X, ALU.add).then_inc(s_slot, 1)
                    v.wait_ge(s_slot, n + 1)

                    def rest(e, kind, slot):
                        m = chunk_no(l, p, e, kind)
                        v.wait_ge(s_hi, m + 1)
                        tt(ring_r[slot][:], ring[slot][:], w_hi[:, slot % 2, :].bitcast(F32), ALU.subtract).then_inc(s_lo, 1)

                    def tokens_rest(e):
                        v.wait_ge(s_xh, n * (NE + 1) + e + 1)
                        for h in range(2):
                            ins = tt(xs_lo[:, 4 * h:4 * h + 4, :], bX[h][:].rearrange("p (k s) -> p k s", k=4),
                                     xs_hi[:, 4 * h:4 * h + 4, :].bitcast(F32), ALU.subtract)
                        ins.then_inc(s_xs, 1)

                    def activate(e, par):
                        tc(gcol[:, par:par + 1], gsl[:, e:e + 1] if isinstance(e, int) else gsl[:, bass.ds(e, 1)]).then_inc(s_gcol, 1)
                        v.wait_ge(s_gcol, n * NE + e + 1)
                        v.wait_ge(s_gu, n * NE + e + 1)
                        v.wait_ge(s_sg, n * NE + e + 1)
                        stt(sa, bU[:], gcol[:, par:par + 1], sa, ALU.mult, ALU.mult).then_inc(s_a, 1)

                    def turned_rest(e):
                        v.wait_ge(s_ah, n * NE + e + 1)
                        tt(aT_lo, bA[:].rearrange("p (k s) -> p k s", k=4), aT_hi.bitcast(F32), ALU.subtract).then_inc(s_as, 1)

                    rest(0, 0, 0)
                    tokens_rest(0)
                    rest(0, 1, 1)
                    activate(0, 0)
                    tokens_rest(1)
                    rest(1, 0, place(0, 0)[0])
                    turned_rest(0)
                    rest(1, 1, place(0, 1)[0])

                    def step(i, u, last=False):
                        e = 2 * i + 1 + u
                        rest(e, 2, place(u, 2)[0])
                        activate(e, 1 - u)
                        tokens_rest(e + 1)
                        if not last:
                            rest(e + 1, 0, place(1 - u, 0)[0])
                        turned_rest(e)
                        if not last:
                            rest(e + 1, 1, place(1 - u, 1)[0])
                    step(0, 0)
                    step(0, 1)
                    with v.Fori(1, NE // 2 - 1) as i:
                        step(i, 0)
                        step(i, 1)
                    step(NE // 2 - 1, 0, last=True)
                    rest(NE, 2, SLOTS - 1)

                experts(0)
                v.wait_ge(s_cnt, l + 1)
                most = v.value_load(cnti[0:1, 0:1], min_val=0, max_val=T)
                for p in range(1, PASSES):
                    with v.If(most > P * p):
                        experts(p)
                    with v.Else():
                        v.wait_ge(s_lo, MOE_CH * (PASSES * l + p))
                        for s, k in ((s_rest, 1), (s_oneh, NG), (s_slot, 1), (s_gcol, NE), (s_xs, NE + 1), (s_lo, MOE_CH),
                                     (s_a, NE), (s_as, NE)):
                            v.sem_inc(s, k)

                def add_rows(t):
                    v.wait_ge(s_yl[t], 16 * TOPK * (l + 1))
                    tt(yl[:, t, 0, :], yl[:, t, 0, :], yl[:, t, 1, :], ALU.add).then_inc(s_ysum, 1)

                add_rows(0)
                for t in range(NT):
                    if t + 1 < NT:
                        add_rows(t + 1)
                    cond = 1 if t == 0 else 0
                    for h in range(2):
                        b = take(v, (l, f"y{t}{h}"))
                        for k in range(4):
                            x = zT[:, 4 * h + k, t * P:(t + 1) * P]
                            ins = stt(x, b[:, k * P:(k + 1) * P], modT[:, l, 40 + 4 * h + k, cond:cond + 1], x, ALU.mult, ALU.add)
                        evac((l, f"y{t}{h}"), ins)
                read_out(v, (l, "y21"))

            feature_sums(2 * DEPTH + 1)
            rsqrt("nfc", D)
            normalise("nfb", None, 0)
            for t in range(NT):
                b = take(v, f"fo{t}1")
                evac(f"fo{t}1", tc(xrows[:, t, 512:1024], b[:]))

        @block.gpsimd
        def _(g):
            g.dma_start(swaf, C_dram[:, KEPT_W:CONST_W]).then_inc(s_swaf, 16)
            bound_h, bound_y = g.to_reg(T - 1), g.to_reg(TOPK * T - 1)
            chain = Chain(g, s_chainp)
            nc.gpsimd.memset(sinks[:], -1e38)
            nc.gpsimd.memset(idxg[:, NE:NE + 1], int(BIG))
            chain(nc.gpsimd.memset(bpad, 0.0))
            for l in range(DEPTH):
                g.dma_start(sinks[:, l, 10:16], A["swa_sink"][l:l + 1, :].to_broadcast([P, SH])).then_inc(s_bs, 16)
            g.dma_start(brt[:], A["b_router"].rearrange("(o e) -> o e", o=1).to_broadcast([P, NE])).then_inc(s_bs, 16)
            g.dma_start(wr[:], A["w_router"].rearrange("(k p) e -> p k e", p=P)).then_inc(s_bs, 16)
            for i in range(DEPTH * NAH):
                g.dma_start(bpad[DRS * i:DRS * (i + 1), GW - NWW:GW + NWW - 1],
                            A["na_rpb"][i // NAH, i % NAH, NWH - GR:NWH + GR - 1, :]).then_inc(s_bp, 16)
            g.wait_ge(s_bp, 16 * DEPTH * NAH)
            nrow = DEPTH * NAH * DRS
            g.dma_start(bscr.rearrange("r (q c) -> r q c", q=GW), bpad[0:nrow, :].unsqueeze(1).to_broadcast([nrow, GW, TW]))\
                .then_inc(s_bscr, 16)

            for l in range(DEPTH):
                is_filled(g, "x21" if l == 0 else (l - 1, "y21"))
                if l == 0:
                    read_out(g, "vecB")
                chain(nc.gpsimd.memset(ckp[:, 0:ND], 0.0))
                for dst, src in ((cnk, A["cache_na_k"][0, l].rearrange("t h d -> t (h d)")), (cck, A["cache_mla_ckv"][0, l]),
                                 (csk, A["cache_swa_k"][0, l].rearrange("t h d -> t (h d)")), (ckp[:, ND:QKD], A["cache_mla_kpe"][0, l]),
                                 (vna[:, 3, :], A["cache_na_v"][0, l].rearrange("t h d -> t (h d)")),
                                 (swv[:, 3, :], A["cache_swa_v"][0, l].rearrange("t h d -> t (h d)"))):
                    g.dma_start(dst, src).then_inc(s_cache, 16)
                g.dma_start(wqb[:], A["w_mla_qb"][l].rearrange("(k p) n -> p k n", p=P)).then_inc(s_lat, 16)
                g.dma_start(wkvb[:], A["w_mla_kvb"][l]).then_inc(s_lat, 16)
                g.wait_ge(s_kr, l + 1)
                read_out(g, (l, "cache2"))
                nc.gpsimd.tensor_copy(mk[ND:QKD, :, :], kpeT[ND:QKD, :].unsqueeze(1).to_broadcast([RD, MH, TK])).then_inc(s_kpr, 1)
                read_out(g, (l, "rows2"))
                for name, src in (("new_na_k", rows_o[:, 0:2 * P]), ("new_mla_ckv", rows_o[:, 2 * P:3 * P]),
                                  ("new_swa_k", rows_o[:, 3 * P:4 * P]), ("new_mla_kpe", rows_o[:, 4 * P:4 * P + RD]),
                                  ("new_na_v", vna[:, 0, :]), ("new_swa_v", swv[:, 0, :])):
                    dst = O[name][0, l]
                    if len(dst.shape) == 3:
                        dst = dst.rearrange("t h d -> t (h d)")
                    g.dma_start(dst, src).then_inc(s_store, 16)
                g.wait_ge(s_bmd, 16 * GR * NAH * (l + 1))
                b3 = bm.rearrange("p h (r c) -> p (h r) c", c=GW)
                g.wait_ge(s_kpr, l + 1)
                nc.gpsimd.tensor_tensor(b3, b3, cv("colmask").unsqueeze(1).to_broadcast([P, 2 * NAH * GR, GW]), ALU.add)\
                    .then_inc(s_bm, 1)

                g.wait_ge(s_bs, 16 * 4)
                g.wait_ge(s_o, 8 * (l + 1))
                nc.gpsimd.memset(wr32[:, :, NE:32], 0.0).then_inc(s_wr, 1)
                nc.gpsimd.tensor_copy(wr32[:, :, 0:NE], wr[:]).then_inc(s_wr, 1)
                g.wait_ge(s_hscr, 16 * NT * (l + 1))

                def experts(p):
                    n = PASSES * l + p
                    g.wait_ge(s_slot, n + 1)

                    for e in range(-2, NE):
                        if e + 2 <= NE:
                            wait(g, s_xt, n * (NE + 1) + max(e + 1, 0))
                            g.indirect_dma_start(grow[:, e % 2, :], None, hscr,
                                                 bass.IndirectOffsetOnAxis(ap=idxg[:, e + 2:e + 3], axis=0),
                                                 bounds_check=bound_h, oob_is_err=False).then_inc(gathers(l, p)[0][e % 2], 16)
                        if e < 0:
                            continue
                        g.wait_ge(s_ys, n * NE + e + 1)
                        g.indirect_dma_start(yscr, bass.IndirectOffsetOnAxis(ap=idxs[:, e:e + 1], axis=0), ysb[:, e % 2, :], None,
                                             bounds_check=bound_y, oob_is_err=False).then_inc(scatters(l, p)[0][e % 2], 16)

                experts(0)
                g.wait_ge(s_cnt, l + 1)
                most = g.value_load(cnti[0:1, 0:1], min_val=0, max_val=T)
                for p in range(1, PASSES):
                    with g.If(most > P * p):
                        experts(p)
                        for k in range(2):
                            g.wait_ge(gathers(l, p)[0][k], G_PASS[k])
                            g.wait_ge(scatters(l, p)[0][k], SC_PASS)
                        g.sem_inc(s_further, 1)
                    with g.Else():
                        g.sem_inc(s_further, 1)


INS = ["x_prompt", "x_sample", "c", "cache_na_k", "cache_na_v", "cache_mla_ckv", "cache_mla_kpe", "cache_swa_k",
       "cache_swa_v", "c_ctx", "w_ada", "b_ada", "g_attn", "w_in", "g_mla_q", "w_mla_qb", "g_mla_kv", "w_mla_kvb", "na_rpb",
       "swa_sink", "w_out", "g_ffn", "w_router", "b_router", "w_gate", "w_up", "w_down", "g_final"]
OUTS = [("y_prompt", (1, TP, D)), ("y_sample", (1, TS, D)), ("new_na_k", (1, DEPTH, TP, NAH, HD)),
        ("new_na_v", (1, DEPTH, TP, NAH, HD)), ("new_mla_ckv", (1, DEPTH, TP, KR)), ("new_mla_kpe", (1, DEPTH, TP, RD)),
        ("new_swa_k", (1, DEPTH, TP, SKV, HD)), ("new_swa_v", (1, DEPTH, TP, SKV, HD))]


def kernel(**inputs):
    import numpy as _np
    import concourse.bacc as _bacc
    from concourse import mybir as _mybir
    from concourse.bass_utils import run_bass_kernel_spmd as _run

    nc = _bacc.Bacc("TRN2", target_bir_lowering=False, num_devices=1)
    arrays, args = {}, {}
    for name in INS:
        a = _np.ascontiguousarray(inputs[name])
        arrays[f"in_{name}"] = a
        args[name] = nc.dram_tensor(f"in_{name}", a.shape, _mybir.dt.from_np(a.dtype), kind="ExternalInput").ap()
    arrays["constants"] = constants()
    consts = nc.dram_tensor("constants", arrays["constants"].shape, F32, kind="ExternalInput").ap()
    outs = {name: nc.dram_tensor(f"out_{name}", shape, F32, kind="ExternalOutput").ap() for name, shape in OUTS}
    build(nc, args, consts, outs)
    r = _run(nc, [arrays], core_ids=[0])
    return tuple(r.results[0][f"out_{name}"] for name, _ in OUTS)
```
